# Optimizing a Trainium2 kernel written in Bass

```python
import math
import jax, jax.numpy as jnp
from jax import lax
import numpy as np

D_MODEL = 1024
BATCH = 1
SEQ = 512
DEPTH = 2
DEC_BATCH = 8
DEC_SEQ = 8
PAST_LEN = 1024
PAGE_SIZE = 128

HEAD_DIM = 64
SWA_WIDTH = D_MODEL // 2
N_Q_HEADS = SWA_WIDTH // HEAD_DIM
N_KV_HEADS = 2
Q_PER_KV = N_Q_HEADS // N_KV_HEADS
KV_WIDTH = N_KV_HEADS * HEAD_DIM
WINDOW = 128
ROPE_THETA = 500000.0
ROT_DIM = HEAD_DIM // 4
POOL_WINDOWS = (2, 4, 8, 16)
N_POOL_GROUPS = 4
POOL_WIDTH = D_MODEL // 4
POOL_GROUP = POOL_WIDTH // N_POOL_GROUPS
POOL_STATE = max(POOL_WINDOWS) - 1
N_MEM = 256
N_X_HEADS = 4
X_WIDTH = N_X_HEADS * HEAD_DIM
N_BRANCH = 3
IN_COLS = POOL_WIDTH + SWA_WIDTH + 2 * KV_WIDTH + X_WIDTH + N_BRANCH * D_MODEL
SPLITS = (POOL_WIDTH,
          POOL_WIDTH + SWA_WIDTH,
          POOL_WIDTH + SWA_WIDTH + KV_WIDTH,
          POOL_WIDTH + SWA_WIDTH + 2 * KV_WIDTH,
          POOL_WIDTH + SWA_WIDTH + 2 * KV_WIDTH + X_WIDTH)
D_FF = 256 * math.ceil(8 * D_MODEL / 3 / 256)
ALPHA = (2 * DEPTH) ** 0.25
BETA = (8 * DEPTH) ** -0.25
LN_EPS = 1e-5

kernel_name = "hybrid_pool_swa_cross_macaron_step"

F32 = jnp.float32

def _layer_norm(x, g, b):
    xf = x.astype(F32)
    mu = jnp.mean(xf, axis=-1, keepdims=True)
    var = jnp.mean(jnp.square(xf - mu), axis=-1, keepdims=True)
    return ((xf - mu) * lax.rsqrt(var + LN_EPS) * g.astype(F32) + b.astype(F32)).astype(x.dtype)

def _swiglu(x, w_gate, w_up, w_down):
    return (jax.nn.silu(x @ w_gate) * (x @ w_up)) @ w_down

def _rope_partial(x, pos):
    half = ROT_DIM // 2
    inv_freq = jnp.power(ROPE_THETA, -jnp.arange(half, dtype=F32) * (2.0 / ROT_DIM))
    ang = pos.astype(F32)[:, None] * inv_freq[None, :]
    cos = jnp.cos(ang)[:, None, :]
    sin = jnp.sin(ang)[:, None, :]
    xr = x[..., :ROT_DIM].astype(F32)
    x1, x2 = xr[..., :half], xr[..., half:]
    rot = jnp.concatenate([x1 * cos - x2 * sin, x2 * cos + x1 * sin], axis=-1).astype(x.dtype)
    return jnp.concatenate([rot, x[..., ROT_DIM:]], axis=-1)

def _sink_attention(q, k, v, sink, mask):
    s = jnp.einsum('...qhgd,...khd->...hgqk', q, k).astype(F32) * (HEAD_DIM ** -0.5)
    s = jnp.where(mask, s, -jnp.inf)
    sink_l = sink.astype(F32).reshape(N_KV_HEADS, Q_PER_KV)[:, :, None, None]
    m = jnp.maximum(jnp.max(s, axis=-1, keepdims=True), sink_l)
    p = jnp.exp(s - m)
    denom = jnp.sum(p, axis=-1, keepdims=True) + jnp.exp(sink_l - m)
    return jnp.einsum('...hgqk,...khd->...qhgd', (p / denom).astype(v.dtype), v)

def _swa_prompt(q, k, v, sink):
    b, s = q.shape[:2]
    nb = s // WINDOW
    qb = q.reshape(b, nb, WINDOW, N_KV_HEADS, Q_PER_KV, HEAD_DIM)
    kb = k.reshape(b, nb, WINDOW, N_KV_HEADS, HEAD_DIM)
    vb = v.reshape(b, nb, WINDOW, N_KV_HEADS, HEAD_DIM)
    pad = jnp.zeros_like(kb[:, :1])
    kk = jnp.concatenate([jnp.concatenate([pad, kb[:, :-1]], axis=1), kb], axis=2)
    vv = jnp.concatenate([jnp.concatenate([pad, vb[:, :-1]], axis=1), vb], axis=2)
    i = jnp.arange(WINDOW)[:, None]
    j = jnp.arange(2 * WINDOW)[None, :]
    rel = i + WINDOW - j
    blk = jnp.arange(nb)[:, None, None]
    mask = (rel >= 0) & (rel < WINDOW) & ((blk > 0) | (j >= WINDOW))
    o = _sink_attention(qb, kk, vv, sink, mask[None, :, None, None])
    return o.reshape(b, s, SWA_WIDTH)

def _swa_sample(q, k, v, cache_k, cache_v, sink, start):
    b, l = q.shape[:2]
    nbuf = cache_k.shape[1]
    kk = jnp.concatenate([cache_k, k], axis=1)
    vv = jnp.concatenate([cache_v, v], axis=1)
    qpos = start + jnp.arange(l)
    kpos = start - nbuf + jnp.arange(nbuf + l)
    rel = qpos[:, None] - kpos[None, :]
    mask = (rel >= 0) & (rel < WINDOW) & (kpos[None, :] >= 0)
    qg = q.reshape(b, l, N_KV_HEADS, Q_PER_KV, HEAD_DIM)
    o = _sink_attention(qg, kk, vv, sink, mask)
    return o.reshape(b, l, SWA_WIDTH), kk[:, -nbuf:], vv[:, -nbuf:]

def _pool_branch(xp, prefix, start, pool_mix, pool_scale):
    b, s, _ = xp.shape
    comb = jnp.concatenate([prefix, xp], axis=1)
    cs = jnp.cumsum(comb.astype(F32), axis=1)
    cs = jnp.concatenate([jnp.zeros((b, 1, POOL_WIDTH), F32), cs], axis=1)
    pos = start + jnp.arange(s)
    means = []
    for g, w in enumerate(POOL_WINDOWS):
        lo, hi = g * POOL_GROUP, (g + 1) * POOL_GROUP
        lead = cs[:, POOL_STATE + 1:POOL_STATE + 1 + s, lo:hi]
        lag = cs[:, POOL_STATE + 1 - w:POOL_STATE + 1 - w + s, lo:hi]
        cnt = jnp.minimum(w, pos + 1).astype(F32)[None, :, None]
        means.append((lead - lag) / cnt)
    mean = jnp.concatenate(means, axis=-1)
    d = (mean - xp.astype(F32)).astype(xp.dtype).reshape(b, s, N_POOL_GROUPS, POOL_GROUP)
    y = jnp.einsum('bsgc,gcd->bsgd', d, pool_mix).reshape(b, s, POOL_WIDTH) * pool_scale
    return y, comb[:, -POOL_STATE:]

def _cross_attention(q, mem_k, mem_v):
    b, s = q.shape[:2]
    sc = jnp.einsum('bshd,bmhd->bhsm', q, mem_k).astype(F32) * (HEAD_DIM ** -0.5)
    p = jax.nn.softmax(sc, axis=-1).astype(mem_v.dtype)
    return jnp.einsum('bhsm,bmhd->bshd', p, mem_v).reshape(b, s, X_WIDTH)

def _layer(x, start, pool_prefix, cache_k, cache_v, mem_k, mem_v,
           ffn1_w_gate, ffn1_w_up, ffn1_w_down, ln1_g, ln1_b,
           w_in, pool_mix, pool_scale, attn_sink, w_br_pool, w_br_swa, w_br_cross, w_o,
           ln2_g, ln2_b, ffn2_w_gate, ffn2_w_up, ffn2_w_down, ln3_g, ln3_b):
    b, s, _ = x.shape
    positions = start + jnp.arange(s)
    x = _layer_norm(ALPHA * x + 0.5 * _swiglu(x, ffn1_w_gate, ffn1_w_up, ffn1_w_down), ln1_g, ln1_b)
    h = x @ w_in
    xp, q, k, v, xq, gates = jnp.split(h, SPLITS, axis=-1)
    q = _rope_partial(q.reshape(b, s, N_Q_HEADS, HEAD_DIM), positions)
    k = _rope_partial(k.reshape(b, s, N_KV_HEADS, HEAD_DIM), positions)
    v = v.reshape(b, s, N_KV_HEADS, HEAD_DIM)
    y_pool, new_pool = _pool_branch(xp, pool_prefix, start, pool_mix, pool_scale)
    if cache_k is None:
        y_swa = _swa_prompt(q, k, v, attn_sink)
        nbuf = min(WINDOW, s)
        new_k, new_v = k[:, -nbuf:], v[:, -nbuf:]
    else:
        y_swa, new_k, new_v = _swa_sample(q, k, v, cache_k, cache_v, attn_sink, start)
    y_x = _cross_attention(xq.reshape(b, s, N_X_HEADS, HEAD_DIM), mem_k, mem_v)
    g = jax.nn.sigmoid(gates.reshape(b, s, N_BRANCH, D_MODEL))
    merged = (g[:, :, 0] * (y_pool @ w_br_pool)
              + g[:, :, 1] * (y_swa @ w_br_swa)
              + g[:, :, 2] * (y_x @ w_br_cross))
    x = _layer_norm(ALPHA * x + merged @ w_o, ln2_g, ln2_b)
    x = _layer_norm(ALPHA * x + 0.5 * _swiglu(x, ffn2_w_gate, ffn2_w_up, ffn2_w_down), ln3_g, ln3_b)
    return x, new_k, new_v, new_pool

def setup_inputs(seed: int = 0) -> dict:
    key = jax.random.key(seed)
    ks = iter(jax.random.split(key, 40))

    def nrm(shape, scale=1.0):
        return jax.random.normal(next(ks), shape, F32) * scale

    d = {}
    d["x_prompt"] = nrm((BATCH, SEQ, D_MODEL))
    d["x_sample"] = nrm((DEC_BATCH, DEC_SEQ, D_MODEL))
    d["cache_swa_k"] = nrm((DEPTH, DEC_BATCH, min(WINDOW, PAST_LEN), N_KV_HEADS, HEAD_DIM))
    d["cache_swa_v"] = nrm((DEPTH, DEC_BATCH, min(WINDOW, PAST_LEN), N_KV_HEADS, HEAD_DIM))
    d["state_pool"] = nrm((DEPTH, DEC_BATCH, POOL_STATE, POOL_WIDTH))
    d["cache_mem_k"] = nrm((DEPTH, DEC_BATCH, N_MEM, N_X_HEADS, HEAD_DIM))
    d["cache_mem_v"] = nrm((DEPTH, DEC_BATCH, N_MEM, N_X_HEADS, HEAD_DIM))
    d["mem_prompt"] = nrm((BATCH, N_MEM, D_MODEL))
    d["w_mem_k"] = nrm((DEPTH, D_MODEL, X_WIDTH), D_MODEL ** -0.5)
    d["w_mem_v"] = nrm((DEPTH, D_MODEL, X_WIDTH), D_MODEL ** -0.5)
    d["ffn1_w_gate"] = nrm((DEPTH, D_MODEL, D_FF), D_MODEL ** -0.5)
    d["ffn1_w_up"] = nrm((DEPTH, D_MODEL, D_FF), D_MODEL ** -0.5)
    d["ffn1_w_down"] = nrm((DEPTH, D_FF, D_MODEL), BETA * D_FF ** -0.5)
    d["ln1_g"] = 1.0 + nrm((DEPTH, D_MODEL), 0.02)
    d["ln1_b"] = nrm((DEPTH, D_MODEL), 0.02)
    d["w_in"] = nrm((DEPTH, D_MODEL, IN_COLS), D_MODEL ** -0.5)
    d["pool_mix"] = nrm((DEPTH, N_POOL_GROUPS, POOL_GROUP, POOL_GROUP), POOL_GROUP ** -0.5)
    d["pool_scale"] = 1.0 + nrm((DEPTH, POOL_WIDTH), 0.1)
    d["attn_sink"] = nrm((DEPTH, N_Q_HEADS), 0.5)
    d["w_br_pool"] = nrm((DEPTH, POOL_WIDTH, D_MODEL), POOL_WIDTH ** -0.5)
    d["w_br_swa"] = nrm((DEPTH, SWA_WIDTH, D_MODEL), SWA_WIDTH ** -0.5)
    d["w_br_cross"] = nrm((DEPTH, X_WIDTH, D_MODEL), X_WIDTH ** -0.5)
    d["w_o"] = nrm((DEPTH, D_MODEL, D_MODEL), BETA * D_MODEL ** -0.5)
    d["ln2_g"] = 1.0 + nrm((DEPTH, D_MODEL), 0.02)
    d["ln2_b"] = nrm((DEPTH, D_MODEL), 0.02)
    d["ffn2_w_gate"] = nrm((DEPTH, D_MODEL, D_FF), D_MODEL ** -0.5)
    d["ffn2_w_up"] = nrm((DEPTH, D_MODEL, D_FF), D_MODEL ** -0.5)
    d["ffn2_w_down"] = nrm((DEPTH, D_FF, D_MODEL), BETA * D_FF ** -0.5)
    d["ln3_g"] = 1.0 + nrm((DEPTH, D_MODEL), 0.02)
    d["ln3_b"] = nrm((DEPTH, D_MODEL), 0.02)
    return d

def reference(x_prompt, x_sample, cache_swa_k, cache_swa_v, state_pool, cache_mem_k, cache_mem_v,
              mem_prompt, w_mem_k, w_mem_v,
              ffn1_w_gate, ffn1_w_up, ffn1_w_down, ln1_g, ln1_b,
              w_in, pool_mix, pool_scale, attn_sink, w_br_pool, w_br_swa, w_br_cross, w_o,
              ln2_g, ln2_b, ffn2_w_gate, ffn2_w_up, ffn2_w_down, ln3_g, ln3_b):
    yp, ys = x_prompt, x_sample
    bp = x_prompt.shape[0]
    pk, pv, pp, pmk, pmv = [], [], [], [], []
    sk, sv, sp = [], [], []
    for l in range(DEPTH):
        lw = (ffn1_w_gate[l], ffn1_w_up[l], ffn1_w_down[l], ln1_g[l], ln1_b[l],
              w_in[l], pool_mix[l], pool_scale[l], attn_sink[l], w_br_pool[l], w_br_swa[l],
              w_br_cross[l], w_o[l], ln2_g[l], ln2_b[l],
              ffn2_w_gate[l], ffn2_w_up[l], ffn2_w_down[l], ln3_g[l], ln3_b[l])
        mk = (mem_prompt @ w_mem_k[l]).reshape(bp, N_MEM, N_X_HEADS, HEAD_DIM)
        mv = (mem_prompt @ w_mem_v[l]).reshape(bp, N_MEM, N_X_HEADS, HEAD_DIM)
        prefix0 = jnp.zeros((bp, POOL_STATE, POOL_WIDTH), yp.dtype)
        yp, nk, nv, npool = _layer(yp, 0, prefix0, None, None, mk, mv, *lw)
        pk.append(nk); pv.append(nv); pp.append(npool); pmk.append(mk); pmv.append(mv)
        ys, nk, nv, npool = _layer(ys, PAST_LEN, state_pool[l], cache_swa_k[l], cache_swa_v[l],
                                   cache_mem_k[l], cache_mem_v[l], *lw)
        sk.append(nk); sv.append(nv); sp.append(npool)
    return (yp, ys,
            jnp.stack(pk), jnp.stack(pv), jnp.stack(pp), jnp.stack(pmk), jnp.stack(pmv),
            jnp.stack(sk), jnp.stack(sv), jnp.stack(sp))


_drawn_inputs = setup_inputs


def setup_inputs(seed=0):
    import zlib

    import numpy as np

    out = dict(_drawn_inputs(seed))
    spreads = {}
    factors = {'attn_sink': 28.533}
    for name, (base, spread) in spreads.items():
        noise = np.random.default_rng([zlib.crc32(name.encode()), seed]).standard_normal(out[name].shape)
        drawn = base * np.exp(spread * noise) if base else spread * noise
        out[name] = __import__('jax').numpy.asarray(drawn.astype(out[name].dtype))
    for name, factor in factors.items():
        out[name] = (out[name] * factor).astype(out[name].dtype)
    return out
```

```python
from contextlib import ExitStack

import concourse.bass as bass
from concourse import mybir

F32 = mybir.dt.float32
F32R = mybir.dt.float32r
ALU = mybir.AluOpType
ACT = mybir.ActivationFunctionType
AX = mybir.AxisListType

L = 2
P = 128
D = 1024
KC = D // P
T_PROMPT = 512
DEC_B, DEC_T = 8, 8
T = T_PROMPT + DEC_B * DEC_T
TH = T // 2
D_FF = 2816
FC = D_FF // P
HD = 64
WIN = 128
N_MEM = 256
N_BLK = T_PROMPT // WIN
POOL_STATE = 15
N_GATE_EARLY = 12
ALPHA = (2 * 2) ** 0.25
LN_EPS = 1e-5
NEG = -1.0e30

PAIR_MEM = 4
Q_GU = {0: 0, 1: 59}
Q_DOWN = {0: 22, 1: 81}
Q_IN = 34
Q_GATES = 39
Q_MERGE = 45
Q_WO = 55
PAIRS = 93

U_MEM = 4
U_GU = {0: 0, 1: 51}
U_DOWN = {0: 22, 1: 73}
U_IN = 26
U_GATES = 31
U_MERGE = 37
U_WO = 47
USES = 77

GROUPS = [("swa_sample",), ("cross_sample",)]
for _n in range(N_BLK):
    GROUPS += [("swa", _n, 0), ("swa", _n, 1), ("cross", _n)]
NG = len(GROUPS)

S_ORDER = ["var0"] + [("rot", i) for i in range(5)]
T_ORDER = ["mean0"]
for _i in range(NG):
    T_ORDER += [("tr", _i - 1)] * (_i > 0)
    S_ORDER += [("scores", _i)]
    T_ORDER += [("pv", _i - 1)] * (_i > 0)
    if _i in (4, 5):
        S_ORDER += [("mix", _i - 4)]
T_ORDER += [("tr", NG - 1), ("pv", NG - 1)]
S_ORDER += [("merge", m) for m in range(KC)] + ["var1", "var2"]
T_ORDER += [("merge", m) for m in range(KC)] + ["mean1", "mean2"]
S_USE = {k: i for i, k in enumerate(S_ORDER)}
T_USE = {k: i for i, k in enumerate(T_ORDER)}
NS, NT = len(S_ORDER), len(T_ORDER)

C_COS, C_SIN, C_ID, C_ROT, C_ONES = 0, T, 2 * T, 2 * T + P, 2 * T + 2 * P
C_MASK = 2 * T + 3 * P
C_MSC = C_MASK + 2 * P
C_MSN = C_MSC + P
C_INVW = C_MSN + 4 * 64
C_TAB = C_INVW + 2
NCST = C_TAB + 32
P_LN, P_MIX, P_SCALE, P_SINK, P_SROW = 0, 48, 48 + 256, 48 + 256 + 2, 48 + 256 + 10
NPAR = P_SROW + 1

XP_P = POOL_STATE + T_PROMPT
XP_S = POOL_STATE + DEC_T
TMP = XP_P + DEC_B * XP_S


def build(nc, wblk, x0, mem0, cst_d, par_d, mks_d, mvs_d, kcs_d, vcs_d, sps_d,
          y_out, kT_out, v_out, poolp_out, pools_out, mk_out, mv_out, kc_out, vc_out):
    with ExitStack() as ctx:
        def sb(name, shape, dt=F32):
            return ctx.enter_context(nc.sbuf_tensor(name, [P] + shape, dt))

        def sem(name):
            return ctx.enter_context(nc.semaphore(name))

        x = sb("x", [KC, T])
        xh, xl = sb("xh", [KC, T], F32R), sb("xl", [KC, T], F32R)
        raw = sb("raw", [2, KC * P])
        wh, wl = sb("wh", [2, KC * P], F32R), sb("wl", [2, KC * P], F32R)
        cst = sb("cst", [NCST])
        par = sb("par", [NPAR])
        tmp = sb("tmp", [4, TMP])
        mk = sb("mk", [2, N_MEM])
        mv = sb("mv", [2, N_MEM])
        small = sb("small", [64])
        eps = sb("eps", [1])
        region_bytes = 2 * FC * T * 4
        room = 2 * KC * T * 4 + N_GATE_EARLY * T * 4 + 2 * KC * T * 4
        base = (nc.sbuf_base + 31) // 32 * 32
        region = ctx.enter_context(nc.sbuf_tensor("region", [P, max(region_bytes, room) // 4], F32))
        assert nc.sbuf_base == base + max(region_bytes, room), (nc.sbuf_base, base)

        def at(name, off, shape, dt=F32):
            return nc.alloc_sbuf_tensor_at(name, [P] + shape, dt, offset=base + off)

        Hh, Hl = at("Hh", 0, [FC * T], F32R), at("Hl", FC * T * 4, [FC * T], F32R)
        yh, yl = at("yh", 0, [KC, T], F32R), at("yl", KC * T * 4, [KC, T], F32R)
        memh, meml = at("memh", 0, [KC, N_MEM], F32R), at("meml", KC * N_MEM * 4, [KC, N_MEM], F32R)
        GB = 2 * KC * T * 4
        gates = at("gates", GB, [N_GATE_EARLY * T])
        mem = at("mem", GB, [KC, N_MEM])
        mtmp = at("mtmp", GB + KC * N_MEM * 4, [L, 4 * N_MEM])
        CB = GB + T * 4
        mcs = at("mcs", CB, [2, DEC_B * N_MEM])
        kcs = at("kcs", CB + 16384, [DEC_B, WIN])
        vcs = at("vcs", CB + 16384 + 4096, [DEC_B, WIN])
        MB = GB + N_GATE_EARLY * T * 4
        mgh, mgl = at("mgh", MB, [KC * T], F32R), at("mgl", MB + KC * T * 4, [KC * T], F32R)
        off = MB
        parts = {}
        for name, n in (("q", 4 * T), ("k", T), ("v", 5 * P), ("xq", 2 * T), ("xpp", 2 * XP_P), ("xps", 2 * DEC_B * XP_S),
                        ("prob", 4 * 256), ("pt", 2 * 512), ("qbd", DEC_B * 64), ("xbd", 2 * DEC_B * 32)):
            parts[name] = at(name, off, [n])
            off += (n * 4 + 31) // 32 * 32
        assert off <= MB + 2 * KC * T * 4
        q = parts["q"][:, :].rearrange("p (g t) -> p g t", g=4)
        k = parts["k"]
        v = parts["v"][:, :].rearrange("p (s c) -> p s c", s=5)
        xq = parts["xq"][:, :].rearrange("p (c t) -> p c t", c=2)
        xpp = parts["xpp"][:, :].rearrange("p (c t) -> p c t", c=2)
        xps = parts["xps"][:, :].rearrange("p (c b t) -> p c b t", c=2, b=DEC_B)
        prob, pt = parts["prob"], parts["pt"]
        qbd = parts["qbd"][:, :].rearrange("p (b r) -> p b r", b=DEC_B)
        xbd = parts["xbd"][:, :].rearrange("p (c b r) -> p c b r", c=2, b=DEC_B)

        pair = [ctx.enter_context(nc.psum_tensor(f"pair{i}", [P, 2, 512], F32)) for i in range(2)]
        S = ctx.enter_context(nc.psum_tensor("S", [P, 2, 512], F32))
        TP = ctx.enter_context(nc.psum_tensor("TP", [P, 2, 512], F32))

        ident = cst[:, C_ID:C_ID + P]
        rot = cst[:, C_ROT:C_ROT + P]
        ones = cst[:, C_ONES:C_ONES + P]

        def halves(t):
            return t[:, :, 0:TH]

        def two(ap):
            return ap.rearrange("p (h t) -> p h t", h=2)

        cst_in, mem_in, x_in, par_in = sem("cst_in"), sem("mem_in"), sem("x_in"), sem("par_in")
        raw_in = [sem("raw_in0"), sem("raw_in1")]
        mem_out, memkv_in = sem("mem_out"), sem("memkv_in")
        caches_in, values_in, state_in = sem("caches_in"), sem("values_in"), sem("state_in")
        stored, final_out = sem("stored"), sem("final_out")
        w_hi, w_lo = sem("w_hi"), sem("w_lo")
        blk_done = sem("blk_done")
        pair_free = [sem("pair_free0"), sem("pair_free1")]
        s_free, t_free = sem("s_free"), sem("t_free")
        x_hi, x_ready = sem("x_hi"), sem("x_ready")
        mem_hi, mem_ready = sem("mem_hi"), sem("mem_ready")
        h_hi, h_split = sem("h_hi"), sem("h_split")
        sum_ready, mean_done, cent = sem("sum_ready"), sem("mean_done"), sem("cent")
        sq_ready, sq_used, std_ready, normed = sem("sq_ready"), sem("sq_used"), sem("std_ready"), sem("normed")
        qraw_ready, rot_done, rope_done = sem("qraw_ready"), sem("rot_done"), sem("rope_done")
        qbd_ready, xbd_ready = sem("qbd_ready"), sem("xbd_ready")
        scores_done, max_ready, exp_done, prob_ready = sem("scores_done"), sem("max_ready"), sem("exp_done"), sem("prob_ready")
        tr_done, pt_half, pv_done, y_hi = sem("tr_done"), sem("pt_half"), sem("pv_done"), sem("y_hi")
        diff_ready, mix_done = sem("diff_ready"), sem("mix_done")
        merge_sum, merge_hi, merge_ready = sem("merge_sum"), sem("merge_hi"), sem("merge_ready")

        block = ctx.enter_context(nc.Block())

        def pq(l, off):
            return l * PAIRS + (PAIR_MEM + off)

        def n_use(l, off):
            return l * USES + (U_MEM + off)

        def s_count(l, name):
            return l * NS + S_USE[name]

        def t_count(l, name):
            return l * NT + T_USE[name]

        def merge_steps():
            out = []
            for mm in range(2):
                out += [(3, mm), (0, 4 + mm), (1, 4 + mm), (2, 4 + mm), (3, 4 + mm)]
            return out

        def merge_order(mm):
            return {0: 0, 4: 1, 1: 2, 5: 3}[mm]

        def score_view(t, kind):
            if kind == "swa_sample":
                if t is S:
                    return t[:, :, 0:384].rearrange("p a (b k) -> p a b k", b=2)
                return t[:, 0:768].rearrange("p (a b k) -> p a b k", a=2, b=2)
            if kind == "cross_sample":
                if t is S:
                    return t[:, 0:1, :].rearrange("p a (b k) -> p a b k", b=2)
                return t[:, 0:512].rearrange("p (a b k) -> p a b k", a=1, b=2)
            if t is S:
                return t[:, :, :].rearrange("p a (b k) -> p a b k", b=2)
            return t[:, :].rearrange("p (a b k) -> p a b k", a=2, b=2)

        def out_parts(i):
            g = GROUPS[i]
            o = TP[:, 0, :]
            if g[0] == "swa":
                a = g[2] * HD
                return [(lambda y: y[a:a + HD, 2:6, g[1] * WIN:(g[1] + 1) * WIN],
                         o[a:a + HD, :].rearrange("p (g t) -> p g t", g=4))]
            if g[0] == "cross":
                return [(lambda y: y[:, 6:8, g[1] * WIN:(g[1] + 1) * WIN],
                         o[:, 0:256].rearrange("p (c t) -> p c t", c=2))]
            if g[0] == "swa_sample":
                return [(lambda y, kv=kv, gg=gg: y[kv * HD:(kv + 1) * HD, 2 + gg, T_PROMPT:T].rearrange("p (b t) -> p b t", b=8),
                         o.rearrange("p (b kv g t) -> p b kv g t", b=8, kv=2, g=4)[kv * HD:(kv + 1) * HD, :, kv, gg, :])
                        for kv in range(2) for gg in range(4)]
            return [(lambda y, c=c, h=h: y[h * HD:(h + 1) * HD, 6 + c, T_PROMPT:T].rearrange("p (b t) -> p b t", b=8),
                     o.rearrange("p (c b h t) -> p c b h t", c=2, b=8, h=4)[h * HD:(h + 1) * HD, c, :, 2 * c + h, :])
                    for c in range(2) for h in range(2)]

        def first_key(group):
            return WIN if group[0] == "swa" and group[1] == 0 else 0

        @block.sync
        def _(sp):
            sp.dma_start(mem[:, :, :], mem0).then_inc(mem_in, 16)
            for s in range(2):
                sp.dma_start(raw[:, s, :], wblk[s, :, :]).then_inc(raw_in[s], 16)
            sp.dma_start(cst[:, :], cst_d).then_inc(cst_in, 16)
            sp.dma_start(x[:, :, :], x0).then_inc(x_in, 16)

            def load_blocks(qq):
                for s in range(2):
                    b = sp.snap(qq * 2 + s)
                    src = wblk[bass.ds(b, 1), :, :].rearrange("o p n -> p (o n)")
                    sp.wait_ge(w_lo, b - 1)
                    sp.dma_start(raw[:, s, :], src).then_inc(raw_in[s], 16)

            with sp.Fori(1, PAIR_MEM + 1) as i:
                load_blocks(i)
            sp.wait_ge(pair_free[1], U_MEM + 1)
            sp.wait_ge(pair_free[0], U_MEM + 1)
            for l in range(L):
                sp.dma_start(mk_out[l], mtmp[:, l, 0:2 * N_MEM]).then_inc(mem_out, 16)
                sp.dma_start(mv_out[l], mtmp[:, l, 2 * N_MEM:]).then_inc(mem_out, 16)
            for l in range(L):
                sp.dma_start(kc_out[l], kcs_d[l].rearrange("p (b k) -> p b k", b=DEC_B)[:, :, DEC_T:WIN]).then_inc(stored, 16)
                sp.dma_start(vc_out[l], vcs_d[l, DEC_T:WIN, :]).then_inc(stored, 16)
            sp.wait_ge(mem_out, 64)
            with sp.Fori(0, L) as l:
                def lay(d):
                    return d[bass.ds(l, 1)].rearrange("o p n -> p (o n)")

                with sp.Fori(1, 12) as i:
                    load_blocks(pq(l, 0) + i)
                src = lay(par_d)
                sp.wait_ge(x_ready, l * 24 + 8)
                sp.dma_start(par[:, :], src).then_inc(par_in, 16)
                with sp.Fori(12, 35) as i:
                    load_blocks(pq(l, 0) + i)
                srcs = [lay(d) for d in (kcs_d, vcs_d, mks_d, mk_out, mv_out)]
                sp.wait_ge(blk_done, pq(l, Q_IN) * 2)
                sp.dma_start(kcs[:, :, :].rearrange("p b k -> p (b k)"), srcs[0]).then_inc(caches_in, 16)
                sp.dma_start(vcs[:, :, :].rearrange("p b k -> p (b k)"), srcs[1]).then_inc(caches_in, 16)
                sp.dma_start(mcs[:, :, :].rearrange("p c k -> p (c k)"), srcs[2]).then_inc(caches_in, 16)
                sp.dma_start(mk[:, :, :].rearrange("p c k -> p (c k)"), srcs[3]).then_inc(memkv_in, 16)
                sp.dma_start(mv[:, :, :].rearrange("p c k -> p (c k)"), srcs[4]).then_inc(memkv_in, 16)
                with nc.allow_non_contiguous_dma(reason="15 columns per sequence"):
                    for c in range(2):
                        src = sps_d[bass.ds(l, 1), :, c, :, :].rearrange("o p b t -> p (o b) t")
                        sp.dma_start(xps[:, c, :, 0:POOL_STATE], src).then_inc(state_in, 16)
                with sp.Fori(35, 40) as i:
                    load_blocks(pq(l, 0) + i)
                src = lay(mvs_d)
                sp.wait_ge(scores_done, l * NG + 2)
                sp.dma_start(mcs[:, :, :].rearrange("p c k -> p (c k)"), src).then_inc(values_in, 16)
                with sp.Fori(40, 44) as i:
                    load_blocks(pq(l, 0) + i)
                dk = kT_out[bass.ds(l, 1)].rearrange("o p n -> p (o n)")
                dvp = v_out[bass.ds(l, 1), 0:P].rearrange("o p n -> p (o n)")
                dvs = v_out[bass.ds(l, 1), P:P + 64].rearrange("o p n -> p (o n)")
                dpp = [poolp_out[bass.ds(l, 1), :, c, :].rearrange("o p t -> p (o t)") for c in range(2)]
                dps = [pools_out[bass.ds(l, 1), :, c, :, :].rearrange("o p b t -> p (o b) t") for c in range(2)]
                sp.wait_ge(rope_done, l * 5 + 5)
                sp.dma_start(dk, k[:, 3 * WIN:T]).then_inc(stored, 16)
                sp.wait_ge(pair_free[1], n_use(l, U_IN + 2) + 2)
                sp.dma_start(dvp, v[:, 3, :]).then_inc(stored, 16)
                sp.dma_start(dvs, v[0:64, 4, :]).then_inc(stored, 16)
                sp.wait_ge(pair_free[0], n_use(l, U_IN + 4) + 2)
                sp.wait_ge(pair_free[1], n_use(l, U_IN + 4) + 2)
                sp.wait_ge(state_in, l * 32 + 32)
                with nc.allow_non_contiguous_dma(reason="15 columns per sequence"):
                    for c in range(2):
                        sp.dma_start(dpp[c], xpp[:, c, T_PROMPT:XP_P]).then_inc(stored, 16)
                        sp.dma_start(dps[c], xps[:, c, :, DEC_T:XP_S]).then_inc(stored, 16)
                with sp.Fori(44, PAIRS + 1) as i:
                    load_blocks(pq(l, 0) + i)
            sp.wait_ge(x_ready, L * 24 + 8)
            sp.dma_start(y_out, x[:, :, :]).then_inc(final_out, 16)
            sp.wait_ge(final_out, 16)
            sp.wait_ge(stored, (4 + 7 * L) * 16)

        @block.scalar
        def _(act):
            act.sem_inc(pair_free[0], 1)
            act.sem_inc(pair_free[1], 1)
            act.sem_inc(s_free, 1)
            act.sem_inc(t_free, 1)

            def round_w(qq, s, first=False):
                act.wait_ge(raw_in[s], (qq + 1) * 16)
                if not first:
                    act.wait_ge(blk_done, qq * 2 + s - 1)
                nc.scalar.activation(wh[:, s, :], raw[:, s, :], ACT.Copy).then_inc(w_hi, 1)

            act.wait_ge(mem_in, 16)
            nc.scalar.activation(memh[:, :, :], mem[:, :, :], ACT.Copy).then_inc(mem_hi, 1)
            for s in range(2):
                round_w(0, s, first=True)
            act.wait_ge(x_in, 16)
            for c in range(KC):
                nc.scalar.activation(xh[:, c, :], x[:, c, :], ACT.Copy).then_inc(x_hi, 1)
            with act.Fori(0, L) as l:
                for what in range(2):
                    for s in range(2):
                        b = l * 4 + (2 * what + s)
                        act.wait_ge(blk_done, b + 1)
                        dst = mtmp[:, bass.ds(l, 1), :].rearrange("p o n -> p (o n)")
                        src = pair[s][:, 0, 0:N_MEM]
                        if what == 0:
                            nc.scalar.activation(dst[:, s * N_MEM:(s + 1) * N_MEM], src, ACT.Copy).then_inc(pair_free[s], 1)
                        else:
                            nc.scalar.activation(
                                dst[:, 2 * N_MEM:].rearrange("p (j f) -> p j f", j=2)[:, :, s * P:(s + 1) * P],
                                src.rearrange("p (j f) -> p j f", j=2), ACT.Copy).then_inc(pair_free[s], 1)
                        round_w(l * 2 + (what + 1), s)

            def ffn(l, f):
                with act.Fori(0, FC) as j:
                    qq = pq(l, Q_GU[f]) + j
                    u = n_use(l, U_GU[f]) + j
                    act.wait_ge(blk_done, qq * 2 + 1)
                    act.wait_ge(pair_free[1], u + 1)
                    nc.scalar.activation(two(tmp[:, 0, 0:T]), halves(pair[0]), ACT.Silu).then_inc(pair_free[0], 1)
                    round_w(qq + 1, 0)
                    round_w(qq + 1, 1)
                    act.wait_ge(pair_free[1], u + 2)
                    nc.scalar.activation(Hh[:, bass.ds(j * T, T)], tmp[:, 1, 0:T], ACT.Copy).then_inc(h_hi, 1)
                with act.Fori(0, 12) as i:
                    for s in range(2):
                        round_w(pq(l, Q_DOWN[f]) + i + 1, s)

            def layer_norm(l, n):
                for c in range(KC):
                    act.wait_ge(cent, l * 24 + n * 8 + c + 1)
                    if c >= 2:
                        act.wait_ge(sq_used, l * 24 + n * 8 + c - 1)
                    nc.scalar.activation(tmp[:, c % 2, 0:T], x[:, c, :], ACT.Square).then_inc(sq_ready, 1)
                act.wait_ge(sq_used, l * 24 + n * 8 + 8)
                nc.scalar.activation(two(tmp[:, 3, 0:T]), halves(S), ACT.Sqrt, bias=eps[:, 0:1]).then_inc(s_free, 1)
                for c in range(KC):
                    act.wait_ge(normed, l * 24 + n * 8 + c + 1)
                    g = par[:, P_LN + 16 * n + c:P_LN + 16 * n + c + 1]
                    b = par[:, P_LN + 16 * n + 8 + c:P_LN + 16 * n + 8 + c + 1]
                    nc.scalar.activation(xh[:, c, :], x[:, c, :], ACT.Identity, bias=b, scale=g)
                    act.drain()
                    nc.scalar.activation(x[:, c, :], x[:, c, :], ACT.Identity, bias=b, scale=g).then_inc(x_hi, 1)

            with act.Fori(0, L) as l:
                ffn(l, 0)
                act.wait_ge(par_in, l * 16 + 16)
                layer_norm(l, 0)

                def in_blk(off, s):
                    act.wait_ge(blk_done, pq(l, Q_IN + off) * 2 + s + 1)

                for i in range(5):
                    in_blk(i // 2, i % 2)
                    if i >= 2:
                        act.wait_ge(rope_done, l * 5 + i - 1)
                    nc.scalar.activation(two(tmp[:, i % 2, 0:T]), halves(pair[i % 2]), ACT.Copy,
                                         scale=HD ** -0.5 if i < 4 else 1.0).then_inc(pair_free[i % 2], 1)
                    round_w(pq(l, Q_IN + 1 + i // 2), i % 2)
                in_blk(2, 1)
                nc.scalar.activation(v[:, 0:4, :], pair[1][:, 0, :].rearrange("p (s c) -> p s c", s=4), ACT.Copy)
                nc.scalar.activation(v[0:64, 4, :], pair[1][0:64, 1, 0:P], ACT.Copy).then_inc(pair_free[1], 1)
                round_w(pq(l, Q_IN + 3), 1)
                for c in range(2):
                    in_blk(3, c)
                    nc.scalar.activation(two(xq[:, c, :]), halves(pair[c]), ACT.Copy, scale=HD ** -0.5).then_inc(pair_free[c], 1)
                    round_w(pq(l, Q_IN + 4), c)

                def softmax_exp(i):
                    kind = GROUPS[i][0]
                    f = first_key(GROUPS[i])
                    act.wait_ge(max_ready, l * NG + i + 1)
                    src = score_view(S if kind in ("cross", "cross_sample") else prob, kind)
                    dst = score_view(prob, kind)
                    na = 1 if kind == "cross_sample" else 2
                    for j in range(2 * na):
                        last = nc.scalar.activation(dst[:, j // 2, j % 2, f:], src[:, j // 2, j % 2, f:], ACT.Exp,
                                                    bias=small[:, j:j + 1], accum_out=small[:, 8 + j:9 + j])
                    if kind in ("cross", "cross_sample"):
                        last.then_inc(s_free, 1)
                        act.drain().then_inc(exp_done, 1)
                    else:
                        nc.scalar.activation(small[:, 16:20], small[:, 4:8], ACT.Exp).then_inc(exp_done, 1)

                def copy_pt(i):
                    kind = GROUPS[i][0]
                    act.wait_ge(tr_done, l * NG + i + 1)
                    if kind == "swa_sample":
                        nc.scalar.activation(pt[:, 0:512], TP[:, 0, :], ACT.Copy)
                        nc.scalar.activation(pt[0:64, 512:1024], TP[0:64, 1, :], ACT.Copy).then_inc(t_free, 1)
                    elif kind == "cross_sample":
                        nc.scalar.activation(pt[:, 0:512], TP[:, 0, :], ACT.Copy).then_inc(t_free, 1)
                    elif first_key(GROUPS[i]):
                        nc.scalar.activation(pt[:, 512:1024], TP[:, 1, :], ACT.Copy).then_inc(t_free, 1)
                    else:
                        nc.scalar.activation(pt[:, :].rearrange("p (a n) -> p a n", a=2), TP[:, :, :], ACT.Copy).then_inc(t_free, 1)

                def out_hi(i):
                    act.wait_ge(pv_done, l * NG + i + 1)
                    for dst, src in out_parts(i):
                        last = nc.scalar.activation(dst(yh), src, ACT.Copy)
                    last.then_inc(y_hi, 1)

                def pool_hi(c):
                    act.wait_ge(mix_done, l * 2 + c + 1)
                    nc.scalar.activation(two(yh[:, c, :]), halves(S), ACT.Copy, scale=par[:, P_SCALE + c:P_SCALE + c + 1]).then_inc(y_hi, 1)

                for i in range(NG):
                    if i in (5, 6):
                        pool_hi(i - 5)
                    if i > 0:
                        copy_pt(i - 1)
                    softmax_exp(i)
                    if i > 0:
                        out_hi(i - 1)
                    if i < 2:
                        in_blk(4, i)
                        nc.scalar.activation(xpp[:, i, POOL_STATE:POOL_STATE + TH], pair[i][:, 0, 0:TH], ACT.Copy)
                        nc.scalar.activation(xpp[:, i, POOL_STATE + TH:XP_P], pair[i][:, 1, 0:T_PROMPT - TH], ACT.Copy)
                        nc.scalar.activation(xps[:, i, :, POOL_STATE:XP_S],
                                             pair[i][:, 1, T_PROMPT - TH:TH].rearrange("p (b t) -> p b t", b=8),
                                             ACT.Copy).then_inc(pair_free[i], 1)
                        round_w(pq(l, Q_GATES), i)
                    else:
                        gi = i - 2
                        act.wait_ge(blk_done, pq(l, Q_GATES) * 2 + gi + 1)
                        nc.scalar.activation(two(gates[:, gi * T:(gi + 1) * T]), halves(pair[gi % 2]), ACT.Tanh,
                                             scale=0.5).then_inc(pair_free[gi % 2], 1)
                        round_w(pq(l, Q_GATES + 1 + gi // 2), gi % 2)
                copy_pt(NG - 1)
                out_hi(NG - 1)

                act.wait_ge(stored, (4 + 7 * (l + 1)) * 16)
                with act.Fori(0, 2) as i:
                    for n, (what, mm) in enumerate(merge_steps()):
                        qq = pq(l, Q_MERGE + n // 2) + i * 5
                        act.wait_ge(blk_done, qq * 2 + n % 2 + 1)
                        if what < 3:
                            m_old = i * 2 + (mm - 4)
                            act.wait_ge(merge_sum, l * 8 + i * 4 + 2 * (mm - 4) + 1)
                            nc.scalar.activation(two(gates[:, bass.ds((m_old * 3 + what) * T, T)]), halves(pair[n % 2]),
                                                 ACT.Tanh, scale=0.5).then_inc(pair_free[n % 2], 1)
                            round_w(qq + 1, n % 2)
                        else:
                            round_w(qq + 1, n % 2)
                            act.wait_ge(merge_sum, l * 8 + i * 4 + merge_order(mm) + 1)
                            m = i * 2 + mm
                            nc.scalar.activation(mgh[:, bass.ds(m * T, T)], tmp[:, merge_order(mm) % 2, 0:T],
                                                 ACT.Copy).then_inc(merge_hi, 1)
                with act.Fori(0, 4) as i:
                    for s in range(2):
                        round_w(pq(l, Q_WO) + i + 1, s)
                layer_norm(l, 1)
                ffn(l, 1)
                layer_norm(l, 2)

        @block.vector
        def _(dve):
            def rest_w(qq, s):
                dve.wait_ge(w_hi, qq * 2 + s + 1)
                nc.vector.tensor_tensor(wl[:, s, :], raw[:, s, :], wh[:, s, :].bitcast(F32), ALU.subtract).then_inc(w_lo, 1)

            nc.vector.memset(eps[:, :], LN_EPS)
            dve.wait_ge(cst_in, 16)
            dve.wait_ge(mem_hi, 1)
            nc.vector.tensor_tensor(meml[:, :, :], mem[:, :, :], memh[:, :, :].bitcast(F32), ALU.subtract).then_inc(mem_ready, 1)
            for s in range(2):
                rest_w(0, s)
            for c in range(KC):
                dve.wait_ge(x_hi, c + 1)
                nc.vector.tensor_tensor(xl[:, c, :], x[:, c, :], xh[:, c, :].bitcast(F32), ALU.subtract).then_inc(x_ready, 1)
            with dve.Fori(1, PAIR_MEM + 1) as i:
                for s in range(2):
                    rest_w(i, s)

            def add_residual(m, s):
                xm = x[:, bass.ds(m, 1), :].rearrange("p o t -> p (o t)")
                nc.vector.scalar_tensor_tensor(out=two(xm), in0=two(xm), scalar=ALPHA, in1=halves(pair[s]),
                                               op0=ALU.mult, op1=ALU.add).then_inc(pair_free[s], 1)
                dve.drain()
                nc.vector.tensor_tensor(tmp[:, 2, 0:T], tmp[:, 2, 0:T], xm, ALU.add)
                dve.drain()

            def ffn(l, f):
                with dve.Fori(0, FC) as j:
                    qq = pq(l, Q_GU[f]) + j
                    u = n_use(l, U_GU[f]) + j
                    rest_w(qq + 1, 0)
                    dve.drain()
                    dve.wait_ge(blk_done, qq * 2 + 2)
                    dve.wait_ge(pair_free[0], u + 2)
                    nc.vector.scalar_tensor_tensor(out=two(tmp[:, 1, 0:T]), in0=two(tmp[:, 0, 0:T]), scalar=0.5,
                                                   in1=halves(pair[1]), op0=ALU.mult, op1=ALU.mult).then_inc(pair_free[1], 1)
                    rest_w(qq + 1, 1)
                    dve.wait_ge(h_hi, l * (2 * FC) + (f * FC + 1) + j)
                    hj = bass.ds(j * T, T)
                    nc.vector.tensor_tensor(Hl[:, hj], tmp[:, 1, 0:T], Hh[:, hj].bitcast(F32), ALU.subtract).then_inc(h_split, 1)
                nc.vector.memset(tmp[:, 2, 0:T], 0.0)
                dve.drain()
                with dve.Fori(0, 4) as i:
                    for n in range(6):
                        qq = pq(l, Q_DOWN[f] + n // 2) + i * 3
                        rest_w(qq + 1, n % 2)
                        if n % 3 == 2:
                            dve.wait_ge(blk_done, qq * 2 + n % 2 + 1)
                            add_residual(i * 2 + n // 3, n // 3)

            def layer_norm(l, n):
                dve.drain().then_inc(sum_ready, 1)
                dve.wait_ge(mean_done, l * 3 + n + 1)
                for c in range(KC):
                    last = nc.vector.tensor_tensor(two(x[:, c, :]), two(x[:, c, :]), halves(TP), ALU.subtract)
                    last.then_inc(cent, 1)
                dve.drain().then_inc(t_free, 1)
                dve.wait_ge(s_free, s_count(l, f"var{n}") + 2)
                nc.vector.reciprocal(tmp[:, 3, 0:T], tmp[:, 3, 0:T])
                dve.drain()
                for c in range(KC):
                    nc.vector.tensor_tensor(x[:, c, :], x[:, c, :], tmp[:, 3, 0:T], ALU.mult).then_inc(normed, 1)
                for c in range(KC):
                    dve.wait_ge(x_hi, (l * 24 + 8) + n * 8 + c + 1)
                    nc.vector.tensor_tensor(xl[:, c, :], x[:, c, :], xh[:, c, :].bitcast(F32), ALU.subtract).then_inc(x_ready, 1)

            with dve.Fori(0, L) as l:
                ffn(l, 0)
                layer_norm(l, 0)
                dve.wait_ge(par_in, l * 16 + 16)
                nc.vector.tensor_scalar(par[:, P_SCALE:P_SCALE + 2], par[:, P_SCALE:P_SCALE + 2], 0.5, None, ALU.mult)
                nc.vector.tensor_scalar(small[:, 32:41], par[:, P_SINK:P_SINK + 9], -1.0, None, ALU.mult)

                nc.vector.memset(xpp[:, :, 0:POOL_STATE], 0.0)
                nc.vector.memset(qbd, 0.0)
                nc.vector.memset(xbd, 0.0)

                def rope(i):
                    dst = q[:, i, :] if i < 4 else k[:, :]
                    dve.drain()
                    dve.wait_ge(rot_done, l * 5 + i + 1)
                    nc.vector.tensor_tensor(dst, tmp[:, i % 2, 0:T], cst[:, C_COS:C_COS + T], ALU.mult)
                    nc.vector.tensor_tensor(two(prob[:, 0:T]), two(cst[:, C_SIN:C_SIN + T]), halves(S), ALU.mult).then_inc(s_free, 1)
                    dve.drain()
                    nc.vector.tensor_tensor(dst, dst, prob[:, 0:T], ALU.add).then_inc(rope_done, 1)

                for i in range(5):
                    rest_w(pq(l, Q_IN + 1 + i // 2), i % 2)
                    if i > 0:
                        rope(i - 1)
                rest_w(pq(l, Q_IN + 3), 1)
                rope(4)
                for kv in range(2):
                    a = kv * HD
                    for g in range(4):
                        last = nc.vector.tensor_copy(qbd[a:a + HD, :, kv * 32 + g * 8:kv * 32 + g * 8 + 8],
                                                     q[a:a + HD, g, T_PROMPT:T].rearrange("p (b t) -> p b t", b=8))
                last.then_inc(qbd_ready, 1)
                rest_w(pq(l, Q_IN + 4), 0)
                rest_w(pq(l, Q_IN + 4), 1)
                for c in range(2):
                    dve.wait_ge(pair_free[c], n_use(l, U_IN + 3) + 2)
                    for h in range(2):
                        a = h * HD
                        last = nc.vector.tensor_copy(xbd[a:a + HD, c, :, (2 * c + h) * 8:(2 * c + h) * 8 + 8],
                                                     xq[a:a + HD, c, T_PROMPT:T].rearrange("p (b t) -> p b t", b=8))
                last.then_inc(xbd_ready, 1)

                def softmax_max(i):
                    kind = GROUPS[i][0]
                    f = first_key(GROUPS[i])
                    dve.wait_ge(scores_done, l * NG + i + 1)
                    s4, p4 = score_view(S, kind), score_view(prob, kind)
                    if kind == "swa":
                        for a in range(2):
                            m = cst[:, C_MASK + f:C_MASK + 2 * P].unsqueeze(1).to_broadcast([P, 2, 2 * P - f])
                            last = nc.vector.tensor_tensor(p4[:, a, :, f:], s4[:, a, :, f:], m, ALU.add)
                        last.then_inc(s_free, 1)
                    elif kind == "swa_sample":
                        for a in range(2):
                            m = cst[:, C_MSC:C_MSC + P].unsqueeze(1).to_broadcast([P, 2, P])
                            nc.vector.tensor_tensor(p4[:, a, :, 0:P], s4[:, a, :, 0:P], m, ALU.add)
                            m = cst[:, C_MSN + a * 128:C_MSN + a * 128 + 128].rearrange("p (b k) -> p b k", b=2)
                            last = nc.vector.tensor_tensor(p4[:, a, :, P:192], s4[:, a, :, P:192], m, ALU.add)
                        last.then_inc(s_free, 1)
                    masked = kind in ("swa", "swa_sample")
                    if masked:
                        dve.drain()
                    src = p4 if masked else s4
                    nj = 2 if kind == "cross_sample" else 4
                    last = nc.vector.tensor_reduce(small[:, 0:nj].rearrange("p (a b) -> p a b", b=2), src[:, :, :, f:],
                                                   AX.X, ALU.max, negate=True)
                    if masked:
                        dve.drain()
                        if kind == "swa":
                            kv = GROUPS[i][2]
                            nc.vector.tensor_tensor(small[:, 0:4], small[:, 0:4], small[:, 32 + 4 * kv:36 + 4 * kv], ALU.min)
                            dve.drain()
                            last = nc.vector.tensor_tensor(small[:, 4:8], small[:, 0:4],
                                                           par[:, P_SINK + 4 * kv:P_SINK + 4 * kv + 4], ALU.add)
                        else:
                            nc.vector.tensor_scalar(small[:, 0:4], small[:, 0:4], small[:, 40:41], None, ALU.min)
                            dve.drain()
                            last = nc.vector.tensor_scalar(small[:, 4:8], small[:, 0:4], par[:, P_SROW:P_SROW + 1], None, ALU.add)
                    last.then_inc(max_ready, 1)

                def softmax_div(i):
                    kind = GROUPS[i][0]
                    f = first_key(GROUPS[i])
                    nj = 2 if kind == "cross_sample" else 4
                    dve.wait_ge(exp_done, l * NG + i + 1)
                    if kind in ("swa", "swa_sample"):
                        nc.vector.tensor_tensor(small[:, 8:12], small[:, 8:12], small[:, 16:20], ALU.add)
                        dve.drain()
                    nc.vector.reciprocal(small[:, 20:20 + nj], small[:, 8:8 + nj])
                    dve.drain()
                    p4 = score_view(prob, kind)
                    for j in range(nj):
                        pj = p4[:, j // 2, j % 2, f:]
                        last = nc.vector.tensor_scalar(pj, pj, small[:, 20 + j:21 + j], 0.5, ALU.mult, ALU.mult)
                    last.then_inc(prob_ready, 1)

                def y_before(i):
                    return l * (NG + 2) + i + max(0, min(2, i - 3))

                def out_lo(i):
                    dve.wait_ge(y_hi, y_before(i) + 1)
                    for dst, src in out_parts(i):
                        last = nc.vector.tensor_tensor(dst(yl), src, dst(yh).bitcast(F32), ALU.subtract)
                    last.then_inc(t_free, 1)

                def pool_lo(c):
                    dve.wait_ge(y_hi, l * (NG + 2) + 4 + 2 * c + 1)
                    nc.vector.scalar_tensor_tensor(out=two(yl[:, c, :]), in0=halves(S), scalar=par[:, P_SCALE + c:P_SCALE + c + 1],
                                                   in1=two(yh[:, c, :]).bitcast(F32), op0=ALU.mult, op1=ALU.subtract).then_inc(s_free, 1)

                for i in range(NG):
                    if i in (5, 6):
                        pool_lo(i - 5)
                    softmax_max(i)
                    softmax_div(i)
                    if i > 0:
                        out_lo(i - 1)
                    rest_w(pq(l, Q_GATES + i // 2), i % 2)
                out_lo(NG - 1)

                with dve.Fori(0, 2) as i:
                    for n, (what, mm) in enumerate(merge_steps()):
                        qq = pq(l, Q_MERGE + n // 2) + i * 5
                        rest_w(qq + 1, n % 2)
                        if what == 3:
                            o = merge_order(mm)
                            m = i * 2 + mm
                            gslot = (i * 2 + mm % 4) * 3
                            acc = tmp[:, o % 2, 0:T]
                            dve.wait_ge(blk_done, qq * 2 + n % 2 + 1)
                            if mm >= 4:
                                dve.wait_ge(pair_free[(n - 1) % 2], n_use(l, U_MERGE + (n - 1) // 2) + i * 5 + 2)
                                dve.wait_ge(pair_free[n % 2], n_use(l, U_MERGE + (n - 2) // 2) + i * 5 + 2)
                            for b, ps in enumerate((S, TP, pair[n % 2])):
                                g = gates[:, bass.ds((gslot + b) * T, T)]
                                out = acc if b == 0 else tmp[:, 3, 0:T]
                                ins = nc.vector.scalar_tensor_tensor(out=two(out), in0=two(g), scalar=1.0, in1=halves(ps),
                                                                     op0=ALU.add, op1=ALU.mult)
                                ins.then_inc((s_free, t_free, pair_free[n % 2])[b], 1)
                                if b:
                                    dve.drain()
                                    ins = nc.vector.tensor_tensor(acc, acc, tmp[:, 3, 0:T], ALU.add)
                                    if b == 2:
                                        ins.then_inc(merge_sum, 1)
                                    else:
                                        dve.drain()
                            dve.wait_ge(merge_hi, l * 8 + i * 4 + o + 1)
                            mt = bass.ds(m * T, T)
                            nc.vector.tensor_tensor(mgl[:, mt], acc, mgh[:, mt].bitcast(F32), ALU.subtract).then_inc(merge_ready, 1)
                nc.vector.memset(tmp[:, 2, 0:T], 0.0)
                dve.drain()
                with dve.Fori(0, 4) as i:
                    for s in range(2):
                        qq = pq(l, Q_WO) + i
                        rest_w(qq + 1, s)
                        dve.wait_ge(blk_done, qq * 2 + s + 1)
                        add_residual(i * 2 + s, s)
                layer_norm(l, 1)
                ffn(l, 1)
                layer_norm(l, 2)

        @block.gpsimd
        def _(pool):
            def windows(c, t0, t1):
                def view(t):
                    return (tmp[:, t, 0:XP_P].unsqueeze(1),
                            tmp[:, t, XP_P:TMP].rearrange("p (b t) -> p b t", b=DEC_B))
                src = (xpp[:, c, :].unsqueeze(1), xps[:, c, :, :])
                w, reach = 1, 0
                out = []
                bufs = [view(t0), view(t1)]
                for step in range(2 if c == 0 else 4):
                    dst = bufs[step % 2]
                    reach += w
                    for d, s in zip(dst, src):
                        n = s.shape[-1]
                        nc.gpsimd.tensor_tensor(d[:, :, reach:n], s[:, :, reach:n], s[:, :, reach - w:n - w], ALU.add)
                    pool.drain()
                    w *= 2
                    src = dst
                return bufs

            pool.wait_ge(cst_in, 16)
            with pool.Fori(0, L) as l:
                pool.wait_ge(rope_done, l * 5 + 5)
                pool.wait_ge(state_in, l * 32 + 32)
                for c in range(2):
                    pool.wait_ge(pair_free[c], n_use(l, U_IN + 4) + 2)
                    bufs = windows(c, 2, 3)
                    dp = tmp[:, c, 0:T_PROMPT]
                    ds_ = tmp[:, c, T_PROMPT:T].rearrange("p (b t) -> p b t", b=DEC_B)
                    for h in range(2):
                        a = slice(h * 64, h * 64 + 64)
                        iv = cst[a, C_INVW + c:C_INVW + c + 1]
                        wp, ws = bufs[h]
                        nc.gpsimd.tensor_scalar(dp[a, :], wp[a, 0, POOL_STATE:XP_P], iv, 0.0, ALU.mult, ALU.add)
                        nc.gpsimd.tensor_scalar(ds_[a], ws[a, :, POOL_STATE:XP_S], iv, 0.0, ALU.mult, ALU.add)
                    pool.drain()
                    for h in range(2):
                        a = slice(h * 64, h * 64 + 64)
                        wp, _ = bufs[h]
                        nc.gpsimd.tensor_tensor(dp[a, 0:16], wp[a, 0, POOL_STATE:POOL_STATE + 16],
                                                cst[a, C_TAB + 16 * c:C_TAB + 16 * c + 16], ALU.mult)
                    pool.drain()
                    nc.gpsimd.tensor_tensor(dp, dp, xpp[:, c, POOL_STATE:XP_P], ALU.subtract)
                    nc.gpsimd.tensor_tensor(ds_, ds_, xps[:, c, :, POOL_STATE:XP_S], ALU.subtract)
                    pool.drain().then_inc(diff_ready, 1)

        @block.tensor
        def _(pe):
            def mm3(out, wt, xt, kk, nk, n_out=2):
                for h in range(n_out):
                    nc.tensor.matmul(out(h), wt[0], xt[0](h), start=(kk == 0), stop=False)
                for h in range(n_out):
                    nc.tensor.matmul(out(h), wt[0], xt[1](h), start=False, stop=False)
                for h in range(n_out):
                    last = nc.tensor.matmul(out(h), wt[1], xt[0](h), start=False, stop=(kk == nk - 1))
                return last

            def wt(s, c):
                return wh[:, s, c * P:(c + 1) * P], wl[:, s, c * P:(c + 1) * P]

            def xs(t, c):
                return lambda h: t[:, c, h * TH:(h + 1) * TH]

            def begin(qq, s, u=None):
                pe.wait_ge(w_lo, qq * 2 + s + 1)
                if u is not None:
                    pe.wait_ge(pair_free[s], u + 1)

            def project(l, qq, s, u, x_from=None):
                begin(qq, s, u)
                for c in range(KC):
                    if x_from is not None:
                        pe.wait_ge(x_ready, x_from + c + 1)
                    last = mm3(lambda h: pair[s][:, h, 0:TH], wt(s, c), (xs(xh, c), xs(xl, c)), c, KC)
                last.then_inc(blk_done, 1)

            pe.wait_ge(mem_ready, 1)
            with pe.Fori(0, L) as l:
                for s in range(2):
                    begin(l * 2, s, l * 2)
                    for c in range(KC):
                        last = mm3(lambda h: pair[s][:, 0, 0:N_MEM], wt(s, c),
                                   (lambda h: memh[:, c, :], lambda h: meml[:, c, :]), c, KC, 1)
                    last.then_inc(blk_done, 1)
                for s in range(2):
                    begin(l * 2 + 1, s, l * 2 + 1)
                    for j in range(2):
                        js = slice(j * P, (j + 1) * P)
                        for c in range(KC):
                            w2 = wt(s, c)
                            last = mm3(lambda h: pair[s][:, 0, js], (memh[:, c, js], meml[:, c, js]),
                                       (lambda h: w2[0], lambda h: w2[1]), c, KC, 1)
                    last.then_inc(blk_done, 1)

            def ffn(l, f):
                with pe.Fori(0, FC) as j:
                    for s in range(2):
                        project(l, pq(l, Q_GU[f]) + j, s, n_use(l, U_GU[f]) + j, l * 24 + (16 * f) if s == 0 else None)
                with pe.Fori(0, 4) as i:
                    pe.wait_ge(h_split, l * (2 * FC) + (f + 1) * FC)
                    for m in range(2):
                        for n in range(3):
                            nb = 3 * m + n
                            s = nb % 2
                            qq = pq(l, Q_DOWN[f] + nb // 2) + i * 3
                            begin(qq, s)
                            if n == 0:
                                pe.wait_ge(pair_free[m], n_use(l, U_DOWN[f]) + i + 1)
                            for c in range(8 if n < 2 else 6):
                                kk = 8 * n + c
                                hx = [lambda h, t=t: t[:, kk * T + h * TH:kk * T + (h + 1) * TH] for t in (Hh, Hl)]
                                last = mm3(lambda h: pair[m][:, h, 0:TH], wt(s, c), hx, kk, FC)
                            last.then_inc(blk_done, 1)

            def layer_norm(l, n):
                pe.wait_ge(sum_ready, l * 3 + n + 1)
                pe.wait_ge(t_free, t_count(l, f"mean{n}") + 1)
                for h in range(2):
                    last = nc.tensor.matmul(TP[:, h, 0:TH], ones, tmp[:, 2, h * TH:(h + 1) * TH], start=True, stop=True)
                last.then_inc(mean_done, 1)
                pe.wait_ge(s_free, s_count(l, f"var{n}") + 1)
                for c in range(KC):
                    pe.wait_ge(sq_ready, l * 24 + n * 8 + c + 1)
                    for h in range(2):
                        last = nc.tensor.matmul(S[:, h, 0:TH], ones, tmp[:, c % 2, h * TH:(h + 1) * TH],
                                                start=(c == 0), stop=(c == KC - 1))
                    last.then_inc(sq_used, 1)

            pe.wait_ge(cst_in, 16)
            with pe.Fori(0, L) as l:
                ffn(l, 0)
                layer_norm(l, 0)

                def rotate(i):
                    pe.wait_ge(pair_free[i % 2], n_use(l, U_IN + i // 2) + 2)
                    pe.wait_ge(s_free, s_count(l, ("rot", i)) + 1)
                    for h in range(2):
                        last = nc.tensor.matmul(S[:, h, 0:TH], rot, tmp[:, i % 2, h * TH:(h + 1) * TH], start=True, stop=True)
                    last.then_inc(rot_done, 1)

                def scores(i):
                    g = GROUPS[i]
                    pe.wait_ge(s_free, s_count(l, ("scores", i)) + 1)
                    s4 = score_view(S, g[0])
                    if g[0] == "swa":
                        _, n, kv = g
                        a = slice(kv * HD, kv * HD + HD)
                        f = first_key(g)
                        for j in range(4):
                            last = nc.tensor.matmul(s4[:, j // 2, j % 2, f:], q[a, j, n * WIN:(n + 1) * WIN],
                                                    k[a, (n - 1) * WIN + f:(n + 1) * WIN], start=True, stop=True)
                    elif g[0] == "cross":
                        pe.wait_ge(memkv_in, l * 32 + 32)
                        for j in range(4):
                            a = slice((j // 2) * HD, (j // 2) * HD + HD)
                            last = nc.tensor.matmul(s4[:, j // 2, j % 2, :], xq[a, j % 2, g[1] * WIN:(g[1] + 1) * WIN],
                                                    mk[a, j % 2, :], start=True, stop=True)
                    elif g[0] == "swa_sample":
                        pe.wait_ge(qbd_ready, l + 1)
                        pe.wait_ge(caches_in, l * 48 + 48)
                        for b in range(DEC_B):
                            t, r = b // 2, (b % 2) * 64
                            o = s4[r:r + 64, t // 2, t % 2, :]
                            nc.tensor.matmul(o[:, 0:P], qbd[:, b, :], kcs[:, b, :], start=True, stop=True)
                            last = nc.tensor.matmul(o[:, P:192], qbd[:, b, :], k[:, T_PROMPT:T], start=True, stop=True)
                    else:
                        pe.wait_ge(xbd_ready, l + 1)
                        for b in range(DEC_B):
                            t, r = b // 4, (b % 4) * 32
                            for c in range(2):
                                last = nc.tensor.matmul(s4[r:r + 32, 0, t, :], xbd[:, c, b, :],
                                                        mcs[:, c, b * N_MEM:(b + 1) * N_MEM], start=(c == 0), stop=(c == 1),
                                                        tile_position=(0, r))
                    last.then_inc(scores_done, 1)

                def transposes(i):
                    g = GROUPS[i]
                    pe.wait_ge(prob_ready, l * NG + i + 1)
                    pe.wait_ge(t_free, t_count(l, ("tr", i)) + 1)
                    p4 = score_view(prob, g[0])
                    if g[0] == "swa_sample":
                        for t in range(4):
                            cols = slice(t * P, (t + 1) * P)
                            nc.tensor.transpose(TP[:, 0, cols], p4[:, t // 2, t % 2, 0:P], ident)
                            last = nc.tensor.transpose(TP[0:64, 1, cols], p4[:, t // 2, t % 2, P:192], ident)
                    elif g[0] == "cross_sample":
                        for t in range(2):
                            for kc in range(2):
                                cols = slice((t * 2 + kc) * P, (t * 2 + kc + 1) * P)
                                last = nc.tensor.transpose(TP[:, 0, cols], p4[:, 0, t, kc * P:(kc + 1) * P], ident)
                    else:
                        for kc in range(first_key(g) // P, 2):
                            for j in range(4):
                                last = nc.tensor.transpose(TP[:, kc, j * P:(j + 1) * P],
                                                           p4[:, j // 2, j % 2, kc * P:(kc + 1) * P], ident)
                    last.then_inc(tr_done, 1)

                def values(i):
                    g = GROUPS[i]
                    pe.wait_ge(t_free, t_count(l, ("pv", i)) + 1)
                    o = TP[:, 0, :]
                    if g[0] == "swa":
                        _, n, kv = g
                        a = slice(kv * HD, kv * HD + HD)
                        k0 = first_key(g) // P
                        for j in range(4):
                            for kc in range(k0, 2):
                                last = nc.tensor.matmul(o[a, j * P:(j + 1) * P], v[:, n - 1 + kc, a],
                                                        pt[:, kc * 512 + j * P:kc * 512 + (j + 1) * P],
                                                        start=(kc == k0), stop=(kc == 1))
                    elif g[0] == "cross":
                        for j in range(4):
                            a = slice((j // 2) * HD, (j // 2) * HD + HD)
                            head = 2 * (j % 2) + j // 2
                            for kc in range(2):
                                last = nc.tensor.matmul(o[a, (j % 2) * P:(j % 2 + 1) * P], mv[:, kc, head * HD:(head + 1) * HD],
                                                        pt[:, kc * 512 + j * P:kc * 512 + (j + 1) * P],
                                                        start=(kc == 0), stop=(kc == 1))
                    elif g[0] == "swa_sample":
                        for b in range(DEC_B):
                            cols = slice(b * 64, (b + 1) * 64)
                            nc.tensor.matmul(o[:, cols], vcs[:, b, :], pt[:, cols], start=True, stop=False)
                            last = nc.tensor.matmul(o[:, cols], v[0:64, 4, :], pt[0:64, 512 + b * 64:512 + (b + 1) * 64],
                                                    start=False, stop=True)
                    else:
                        pe.wait_ge(values_in, l * 16 + 16)
                        for b in range(DEC_B):
                            for c in range(2):
                                for kc in range(2):
                                    col = ((b // 4) * 2 + kc) * P + (b % 4) * 32
                                    last = nc.tensor.matmul(o[:, (c * 8 + b) * 32:(c * 8 + b + 1) * 32],
                                                            mcs[:, kc, b * N_MEM + c * P:b * N_MEM + (c + 1) * P],
                                                            pt[:, col:col + 32], start=(kc == 0), stop=(kc == 1))
                    last.then_inc(pv_done, 1)

                def mix(c):
                    pe.wait_ge(par_in, l * 16 + 16)
                    pe.wait_ge(diff_ready, l * 2 + c + 1)
                    pe.wait_ge(s_free, s_count(l, ("mix", c)) + 1)
                    for h in range(2):
                        last = nc.tensor.matmul(S[:, h, 0:TH], par[:, P_MIX + c * P:P_MIX + (c + 1) * P],
                                                tmp[:, c, h * TH:(h + 1) * TH], start=True, stop=True)
                    last.then_inc(mix_done, 1)

                for i in range(5):
                    project(l, pq(l, Q_IN + i // 2), i % 2, n_use(l, U_IN + i // 2), l * 24 + 8 if i == 0 else None)
                    if i > 0:
                        rotate(i - 1)
                begin(pq(l, Q_IN + 2), 1, n_use(l, U_IN + 2))
                for t in range(5):
                    n = P if t < 4 else T - T_PROMPT
                    o = pair[1][0:n, 0, t * P:(t + 1) * P] if t < 4 else pair[1][0:n, 1, 0:P]
                    for c in range(KC):
                        w2 = wt(1, c)
                        xc = xh[:, c, t * P:t * P + n], xl[:, c, t * P:t * P + n]
                        last = mm3(lambda h: o, xc, (lambda h: w2[0], lambda h: w2[1]), c, KC, 1)
                last.then_inc(blk_done, 1)
                rotate(4)
                for c in range(2):
                    project(l, pq(l, Q_IN + 3), c, n_use(l, U_IN + 3))
                for i in range(NG):
                    if i > 0:
                        transposes(i - 1)
                    scores(i)
                    if i < 2:
                        project(l, pq(l, Q_IN + 4), i, n_use(l, U_IN + 4))
                    else:
                        project(l, pq(l, Q_GATES + (i - 2) // 2), i % 2, n_use(l, U_GATES + (i - 2) // 2))
                    if i > 0:
                        values(i - 1)
                    if i in (4, 5):
                        mix(i - 4)
                transposes(NG - 1)
                values(NG - 1)
                with pe.Fori(0, 2) as i:
                    for n, (what, mm) in enumerate(merge_steps()):
                        s = n % 2
                        qq = pq(l, Q_MERGE + n // 2) + i * 5
                        u = n_use(l, U_MERGE + n // 2) + i * 5
                        if what < 3:
                            project(l, qq, s, u)
                            continue
                        begin(qq, s, u)
                        if n == 0:
                            pe.wait_ge(t_free, t_count(l, ("pv", NG - 1)) + 2)
                            pe.wait_ge(s_free, s_count(l, ("mix", 1)) + 2)
                        o = merge_order(mm)
                        for dst, tiles in ((pair[s], (6, 7)), (S, (0, 1)), (TP, (2, 3, 4, 5))):
                            if dst is S:
                                pe.wait_ge(s_free, l * NS + (S_USE[("merge", o)] + 1) + i * 4)
                            if dst is TP:
                                pe.wait_ge(t_free, l * NT + (T_USE[("merge", o)] + 1) + i * 4)
                            for j, c in enumerate(tiles):
                                last = mm3(lambda h: dst[:, h, 0:TH], wt(s, c), (xs(yh, c), xs(yl, c)), j, len(tiles))
                        last.then_inc(blk_done, 1)
                with pe.Fori(0, 4) as i:
                    pe.wait_ge(merge_ready, l * 8 + 8)
                    for s in range(2):
                        begin(pq(l, Q_WO) + i, s, n_use(l, U_WO) + i)
                        for c in range(KC):
                            hx = [lambda h, t=t: t[:, c * T + h * TH:c * T + (h + 1) * TH] for t in (mgh, mgl)]
                            last = mm3(lambda h: pair[s][:, h, 0:TH], wt(s, c), hx, c, KC)
                        last.then_inc(blk_done, 1)
                layer_norm(l, 1)
                ffn(l, 1)
                layer_norm(l, 2)


def _tiles(w, cols, np):
    return w[:, cols].reshape(-1, P, P).transpose(1, 0, 2).reshape(P, -1)


def pack_weights(a, np):
    perm = np.array([(kv * 4 + g) * HD + d for g in range(4) for kv in range(2) for d in range(HD)])
    blocks = []
    for l in range(L):
        for w in (a["w_mem_k"][l], a["w_mem_v"][l]):
            blocks += [_tiles(w, slice(c * P, (c + 1) * P), np) for c in range(2)]
    pad = np.zeros((2 * P, P), np.float32)
    for l in range(L):
        def ffn(name):
            out = []
            for j in range(FC):
                for w in (a[name + "_w_gate"][l], a[name + "_w_up"][l]):
                    out.append(_tiles(w, slice(j * P, (j + 1) * P), np))
            for m in range(KC):
                w = np.concatenate([a[name + "_w_down"][l][:, m * P:(m + 1) * P], pad])
                out += [_tiles(w[n * 8 * P:(n + 1) * 8 * P], slice(0, P), np) for n in range(3)]
            return out
        blocks += ffn("ffn1")
        w = a["w_in"][l]
        pool, swq, k, v, xq, gate = np.split(w, [256, 768, 896, 1024, 1280], axis=1)
        early = [gate[:, b * D + m * P:b * D + (m + 1) * P] for m in range(4) for b in range(3)]
        for w in [swq[:, perm], k, v, xq, pool] + early:
            blocks += [_tiles(w, slice(c * P, (c + 1) * P), np) for c in range(w.shape[1] // P)]
        br = np.concatenate([a["w_br_pool"][l], a["w_br_swa"][l][perm], a["w_br_cross"][l]])
        for i in range(2):
            for mm in range(2):
                m = 2 * i + mm
                blocks.append(_tiles(br, slice(m * P, (m + 1) * P), np))
                for b in range(3):
                    blocks.append(_tiles(gate, slice(b * D + (m + 4) * P, b * D + (m + 5) * P), np))
                blocks.append(_tiles(br, slice((m + 4) * P, (m + 5) * P), np))
        blocks += [_tiles(a["w_o"][l], slice(m * P, (m + 1) * P), np) for m in range(KC)]
        blocks += ffn("ffn2")
    blocks += [np.zeros((P, KC * P), np.float32)] * 2
    assert len(blocks) == 2 * (PAIR_MEM + L * PAIRS + 1)
    return np.stack(blocks)


def constants(np):
    f = np.float32
    c = np.zeros((P, NCST), f)
    pos = np.concatenate([np.arange(T_PROMPT), np.tile(1024 + np.arange(DEC_T), DEC_B)]).astype(f)
    inv = np.power(f(500000.0), -np.arange(8, dtype=f) * f(2.0 / 16)).astype(f)
    ang = (pos[None, :] * inv[:, None]).astype(f)
    p = np.arange(P)
    d = p % HD
    c[:, C_COS:C_COS + T] = 1.0
    for r in range(P):
        if d[r] < 16:
            c[r, C_COS:C_COS + T] = np.cos(ang[d[r] % 8])
            c[r, C_SIN:C_SIN + T] = np.sin(ang[d[r] % 8]) * (-1 if d[r] < 8 else 1)
            c[r + (8 if d[r] < 8 else -8), C_ROT + r] = 1.0
    c[:, C_ID:C_ID + P] = np.eye(P)
    c[:, C_ONES:C_ONES + P] = 1.0 / D
    j = np.arange(P)[None, :]
    i = p[:, None]
    c[:, C_MASK:C_MASK + P] = np.where(j > i, 0, NEG)
    c[:, C_MASK + P:C_MASK + 2 * P] = np.where(j <= i, 0, NEG)
    t = (p % 8)[:, None]
    b = (p // 64)[:, None]
    c[:, C_MSC:C_MSC + P] = np.where(j > t, 0, NEG)
    for tile in range(4):
        kb, kt = np.arange(64)[None, :] // 8, np.arange(64)[None, :] % 8
        c[:, C_MSN + tile * 64:C_MSN + (tile + 1) * 64] = np.where((kb == 2 * tile + b) & (kt <= t), 0, NEG)
    for ch in range(2):
        w = np.where(p < 64, 2, 4) * (4 if ch else 1)
        c[:, C_INVW + ch] = 1.0 / w
        c[:, C_TAB + 16 * ch:C_TAB + 16 * ch + 16] = 1.0 / np.minimum(w[:, None], np.arange(16)[None, :] + 1)
    return c


def kernel(**inputs):
    import numpy as np
    import concourse.bacc as bacc
    from concourse.bass_utils import run_bass_kernel_spmd as run

    a = {n: np.asarray(v) for n, v in inputs.items()}

    def fm(x):
        return x.reshape(x.shape[0], -1, P).transpose(2, 1, 0)

    xs = a["x_sample"].reshape(DEC_B * DEC_T, D)
    par = np.zeros((L, P, NPAR), np.float32)
    for l in range(L):
        for n in range(3):
            for j, w in enumerate("gb"):
                par[l, :, 16 * n + 8 * j:16 * n + 8 * j + 8] = a[f"ln{n + 1}_{w}"][l].reshape(KC, P).T
        for c in range(2):
            for h in range(2):
                par[l, h * 64:h * 64 + 64, P_MIX + c * P + h * 64:P_MIX + c * P + h * 64 + 64] = a["pool_mix"][l, 2 * c + h]
        par[l, :, P_SCALE:P_SCALE + 2] = a["pool_scale"][l].reshape(2, P).T
        par[l, :, P_SINK:P_SINK + 8] = a["attn_sink"][l][None, :]
        par[l, :, P_SROW] = a["attn_sink"][l][(np.arange(P) // 8) % 8]
    mk = a["cache_mem_k"].reshape(L, DEC_B, N_MEM, 2, P)
    mv = a["cache_mem_v"].reshape(L, DEC_B, 2, P, 256)
    kc = a["cache_swa_k"].reshape(L, DEC_B, WIN, P)
    vc = a["cache_swa_v"].reshape(L, DEC_B, WIN, P)
    sp = a["state_pool"].reshape(L, DEC_B, POOL_STATE, 2, P)
    arrays = {
        "wblk": pack_weights(a, np),
        "x0": np.concatenate([fm(a["x_prompt"][0]), fm(xs)], axis=2),
        "mem0": fm(a["mem_prompt"][0]),
        "cst": constants(np),
        "par": par,
        "mks": mk.transpose(0, 4, 3, 1, 2).reshape(L, P, -1),
        "mvs": mv.transpose(0, 3, 2, 1, 4).reshape(L, P, -1),
        "kcs": kc.transpose(0, 3, 1, 2).reshape(L, P, -1),
        "vcs": vc.transpose(0, 2, 1, 3).reshape(L, P, -1),
        "sps": sp.transpose(0, 4, 3, 1, 2),
    }
    arrays = {n: np.ascontiguousarray(v) for n, v in arrays.items()}
    outs = {
        "y": (P, KC, T), "kT": (L, P, P + 64), "v": (L, P + 64, P), "poolp": (L, P, 2, POOL_STATE),
        "pools": (L, P, 2, DEC_B, POOL_STATE), "mk_out": (L, P, 512), "mv_out": (L, P, 512),
        "kc_out": (L, P, DEC_B, WIN - DEC_T), "vc_out": (L, WIN - DEC_T, DEC_B * P),
    }
    nc = bacc.Bacc("TRN2", target_bir_lowering=False, num_devices=1)
    args = [nc.dram_tensor("in_" + n, v.shape, F32, kind="ExternalInput").ap() for n, v in arrays.items()]
    args += [nc.dram_tensor("out_" + n, s, F32, kind="ExternalOutput").ap() for n, s in outs.items()]
    build(nc, *args)
    r = run(nc, [{"in_" + n: v for n, v in arrays.items()}], core_ids=[0]).results[0]
    r = {n: r["out_" + n] for n in outs}

    y = r["y"].transpose(2, 1, 0).reshape(T, D)
    kT = r["kT"].transpose(0, 2, 1)
    v = r["v"]
    pools = r["pools"].transpose(0, 3, 4, 2, 1).reshape(L, DEC_B, POOL_STATE, 256)
    kco = r["kc_out"].transpose(0, 2, 3, 1)
    vco = r["vc_out"].reshape(L, WIN - DEC_T, DEC_B, P).transpose(0, 2, 1, 3)
    return (
        y[:T_PROMPT][None], y[T_PROMPT:].reshape(DEC_B, DEC_T, D),
        kT[:, :P].reshape(L, 1, WIN, 2, HD), v[:, :P].reshape(L, 1, WIN, 2, HD),
        r["poolp"].transpose(0, 3, 2, 1).reshape(L, 1, POOL_STATE, 256),
        r["mk_out"].reshape(L, P, 2, N_MEM).transpose(0, 3, 2, 1).reshape(L, 1, N_MEM, 4, HD),
        r["mv_out"].reshape(L, P, 2, 256).transpose(0, 2, 1, 3).reshape(L, 1, N_MEM, 4, HD),
        np.concatenate([kco, kT[:, P:].reshape(L, DEC_B, DEC_T, P)], axis=2).reshape(L, DEC_B, WIN, 2, HD),
        np.concatenate([vco, v[:, P:].reshape(L, DEC_B, DEC_T, P)], axis=2).reshape(L, DEC_B, WIN, 2, HD),
        pools,
    )
```

```python
from contextlib import ExitStack

import concourse.bass as bass
from concourse import mybir

F32 = mybir.dt.float32
F32R = mybir.dt.float32r
ALU = mybir.AluOpType
ACT = mybir.ActivationFunctionType
AX = mybir.AxisListType

L = 2
P = 128
D = 1024
KC = D // P
T_PROMPT = 512
DEC_B, DEC_T = 8, 8
T = T_PROMPT + DEC_B * DEC_T
TH = T // 2
D_FF = 2816
FC = D_FF // P
HD = 64
WIN = 128
N_MEM = 256
N_BLK = T_PROMPT // WIN
POOL_STATE = 15
N_GATE_EARLY = 12
ALPHA = (2 * 2) ** 0.25
LN_EPS = 1e-5
NEG = -1.0e30
BY_POOL = (1, 3, 5, 6)
BY_DVE = tuple(c for c in range(KC) if c not in BY_POOL)

PAIR_MEM = 4
Q_GU = {0: 0, 1: 59}
Q_DOWN = {0: 22, 1: 81}
Q_IN = 34
Q_GATES = 39
Q_MERGE = 45
Q_WO = 55
PAIRS = 93

MERGE_STEPS = [(3, 0), (0, 4), (1, 4), (3, 1), (2, 4), (0, 5), (3, 4), (1, 5), (2, 5), (3, 5)]
MERGED = (0, 1, 4, 5, 2, 3, 6, 7)

U_MEM = 4
U_GU = {0: 0, 1: 51}
U_DOWN = {0: 22, 1: 73}
U_IN = 26
U_GATES = 31
U_MERGE = 37
U_WO = 47
USES = 77

GROUPS = [("swa_sample",), ("cross_sample",)]
for _n in range(N_BLK):
    GROUPS += [("swa", _n, 0), ("swa", _n, 1), ("cross", _n)]
NG = len(GROUPS)

S_ORDER = ["var0"] + [("rot", i) for i in range(5)]
T_ORDER = ["mean0", "v"]
S_ORDER += [("scores", 0)]
for _i in range(NG):
    S_ORDER += [("scores", _i + 1)] * (_i + 1 < NG)
    T_ORDER += [("tr", _i), ("pv", _i)]
    if _i in (4, 5):
        S_ORDER += [("mix", _i - 4)]
S_ORDER += [("merge", m) for m in range(KC)] + ["var1", "var2"]
T_ORDER += [("merge", m) for m in range(KC)] + ["mean1", "mean2"]
S_USE = {k: i for i, k in enumerate(S_ORDER)}
T_USE = {k: i for i, k in enumerate(T_ORDER)}
NS, NT = len(S_ORDER), len(T_ORDER)

C_COS, C_SIN, C_ID, C_ROT, C_ONES = 0, T, 2 * T, 2 * T + P, 2 * T + 2 * P
C_MASK = 2 * T + 3 * P
C_MSC = C_MASK + 2 * P
C_MSN = C_MSC + P
C_INVW = C_MSN + 4 * 64
C_TAB = C_INVW + 2
NCST = C_TAB + 32
P_LN, P_MIX, P_SCALE, P_SINK, P_SROW = 0, 48, 48 + 256, 48 + 256 + 2, 48 + 256 + 10
NPAR = P_SROW + 1

XP_P = POOL_STATE + T_PROMPT
XP_S = POOL_STATE + DEC_T
TMP = XP_P + DEC_B * XP_S


def build(nc, wblk, x0, mem0, cst_d, par_d, mks_d, mvs_d, kcs_d, vcs_d, sps_d,
          y_out, kT_out, v_out, poolp_out, pools_out, mk_out, mv_out, kc_out, vc_out):
    with ExitStack() as ctx:
        def sb(name, shape, dt=F32):
            return ctx.enter_context(nc.sbuf_tensor(name, [P] + shape, dt))

        def sem(name):
            return ctx.enter_context(nc.semaphore(name))

        x = sb("x", [KC, T])
        xh, xl = sb("xh", [KC, T], F32R), sb("xl", [KC, T], F32R)
        raw = sb("raw", [2, KC * P])
        wh, wl = sb("wh", [2, KC * P], F32R), sb("wl", [2, KC * P], F32R)
        cst = sb("cst", [NCST])
        par = sb("par", [NPAR])
        tmp = sb("tmp", [4, TMP])
        mk = sb("mk", [2, N_MEM])
        mv = sb("mv", [2, N_MEM])
        small = sb("small", [64])
        eps = sb("eps", [1])
        prob1 = sb("prob1", [4 * 256])
        region_bytes = 2 * FC * T * 4
        room = 2 * KC * T * 4 + N_GATE_EARLY * T * 4 + 2 * KC * T * 4
        base = (nc.sbuf_base + 31) // 32 * 32
        region = ctx.enter_context(nc.sbuf_tensor("region", [P, max(region_bytes, room) // 4], F32))
        assert nc.sbuf_base == base + max(region_bytes, room), (nc.sbuf_base, base)

        def at(name, off, shape, dt=F32):
            return nc.alloc_sbuf_tensor_at(name, [P] + shape, dt, offset=base + off)

        Hh, Hl = at("Hh", 0, [FC * T], F32R), at("Hl", FC * T * 4, [FC * T], F32R)
        yh, yl = at("yh", 0, [KC, T], F32R), at("yl", KC * T * 4, [KC, T], F32R)
        memh, meml = at("memh", 0, [KC, N_MEM], F32R), at("meml", KC * N_MEM * 4, [KC, N_MEM], F32R)
        GB = 2 * KC * T * 4
        gates = at("gates", GB, [N_GATE_EARLY * T])
        mem = at("mem", GB, [KC, N_MEM])
        mtmp = at("mtmp", GB + KC * N_MEM * 4, [L, 4 * N_MEM])
        CB = GB + T * 4
        mcs = at("mcs", CB, [2, DEC_B * N_MEM])
        kcs = at("kcs", CB + 16384, [DEC_B, WIN])
        vcs = at("vcs", CB + 16384 + 4096, [DEC_B, WIN])
        MB = GB + N_GATE_EARLY * T * 4
        mgh, mgl = at("mgh", MB, [KC * T], F32R), at("mgl", MB + KC * T * 4, [KC * T], F32R)
        off = MB
        parts = {}
        for name, n in (("q", 4 * T), ("k", T), ("v", 5 * P), ("xq", 2 * T), ("xpp", 2 * XP_P), ("xps", 2 * DEC_B * XP_S),
                        ("prob0", 4 * 256), ("pt", 2 * 512), ("qbd", DEC_B * 64), ("xbd", 2 * DEC_B * 32)):
            parts[name] = at(name, off, [n])
            off += (n * 4 + 31) // 32 * 32
        assert off <= MB + 2 * KC * T * 4
        q = parts["q"][:, :].rearrange("p (g t) -> p g t", g=4)
        k = parts["k"]
        v = parts["v"][:, :].rearrange("p (s c) -> p s c", s=5)
        xq = parts["xq"][:, :].rearrange("p (c t) -> p c t", c=2)
        xpp = parts["xpp"][:, :].rearrange("p (c t) -> p c t", c=2)
        xps = parts["xps"][:, :].rearrange("p (c b t) -> p c b t", c=2, b=DEC_B)
        pt = parts["pt"]
        prob = [parts["prob0"], prob1]
        qbd = parts["qbd"][:, :].rearrange("p (b r) -> p b r", b=DEC_B)
        xbd = parts["xbd"][:, :].rearrange("p (c b r) -> p c b r", c=2, b=DEC_B)

        pair = [ctx.enter_context(nc.psum_tensor(f"pair{i}", [P, 2, 512], F32)) for i in range(2)]
        S = ctx.enter_context(nc.psum_tensor("S", [P, 2, 512], F32))
        TP = ctx.enter_context(nc.psum_tensor("TP", [P, 2, 512], F32))

        ident = cst[:, C_ID:C_ID + P]
        rot = cst[:, C_ROT:C_ROT + P]
        ones = cst[:, C_ONES:C_ONES + P]

        def halves(t):
            return t[:, :, 0:TH]

        def two(ap):
            return ap.rearrange("p (h t) -> p h t", h=2)

        cst_in, x_in, par_in = sem("cst_in"), sem("x_in"), sem("par_in")
        mem_in = [sem("mem_in0"), sem("mem_in1")]
        raw_in = [sem("raw_in0"), sem("raw_in1")]
        mem_out, memkv_in = sem("mem_out"), sem("memkv_in")
        caches_in, values_in, state_in = sem("caches_in"), sem("values_in"), sem("state_in")
        stored, final_out = sem("stored"), sem("final_out")
        w_hi, w_lo = sem("w_hi"), sem("w_lo")
        blk_done = sem("blk_done")
        pair_free = [sem("pair_free0"), sem("pair_free1")]
        s_free, t_free = sem("s_free"), sem("t_free")
        x_hi = sem("x_hi")
        x_lo, x_lo_p = sem("x_lo"), sem("x_lo_p")
        x_full = sem("x_full")
        mem_hi, mem_ready = sem("mem_hi"), sem("mem_ready")
        h_hi, h_split = sem("h_hi"), sem("h_split")
        half_done = sem("half_done")
        sum_ready, mean_done, cent = sem("sum_ready"), sem("mean_done"), sem("cent")
        sq_ready, sq_used, std_ready, normed = sem("sq_ready"), sem("sq_used"), sem("std_ready"), sem("normed")
        rot_done, rope_done, v_done = sem("rot_done"), sem("rope_done"), sem("v_done")
        qbd_ready, xbd_ready = sem("qbd_ready"), sem("xbd_ready")
        scores_done, max_ready, exp_done, prob_ready = sem("scores_done"), sem("max_ready"), sem("exp_done"), sem("prob_ready")
        tr_done, pv_done, y_hi = sem("tr_done"), sem("pv_done"), sem("y_hi")
        diff_ready, mix_done = sem("diff_ready"), sem("mix_done")
        merge_sum, merge_hi, merge_ready = sem("merge_sum"), sem("merge_hi"), sem("merge_ready")

        small_set = sem("small_set")

        block = ctx.enter_context(nc.Block())

        def pq(l, off):
            return l * PAIRS + (PAIR_MEM + off)

        def n_use(l, off):
            return l * USES + (U_MEM + off)

        def s_count(l, name):
            return l * NS + S_USE[name]

        def t_count(l, name):
            return l * NT + T_USE[name]

        def x_hi_count(l, n, h, c):
            return l * (3 * 2 * KC) + (n * 2 * KC + h * KC + c + 1)

        def norm_count(l, n, h, c):
            return l * (3 * 2 * KC) + (n * 2 * KC + h * KC + c + 1)

        def x_split(l, n, h, c):
            if c in BY_POOL:
                m = len(BY_POOL)
                return x_lo_p, l * (6 * m) + (n * 2 * m + h * m + BY_POOL.index(c) + 1)
            m = len(BY_DVE)
            return x_lo, l * (6 * m) + (n * 2 * m + h * m + BY_DVE.index(c) + 1)

        def x_full_count(l, n):
            m = 2 * len(BY_DVE)
            return l * (3 * m) + (n * m + 1)

        def squares(h, c):
            return tmp[:, c % 2, half(c // 2 % 2)]

        def half(h):
            return slice(h * TH, (h + 1) * TH)

        def merge_order(mm):
            return MERGED.index(mm)

        def score_view(t, kind):
            if kind == "swa_sample":
                if t is S:
                    return t[:, :, 0:384].rearrange("p a (b k) -> p a b k", b=2)
                return t[:, 0:768].rearrange("p (a b k) -> p a b k", a=2, b=2)
            if kind == "cross_sample":
                if t is S:
                    return t[:, 0:1, :].rearrange("p a (b k) -> p a b k", b=2)
                return t[:, 0:512].rearrange("p (a b k) -> p a b k", a=1, b=2)
            if t is S:
                return t[:, :, :].rearrange("p a (b k) -> p a b k", b=2)
            return t[:, :].rearrange("p (a b k) -> p a b k", a=2, b=2)

        def out_parts(i):
            g = GROUPS[i]
            o = TP[:, 0, :]
            if g[0] == "swa":
                a = g[2] * HD
                return [(lambda y: y[a:a + HD, 2:6, g[1] * WIN:(g[1] + 1) * WIN],
                         o[a:a + HD, :].rearrange("p (g t) -> p g t", g=4))]
            if g[0] == "cross":
                return [(lambda y: y[:, 6:8, g[1] * WIN:(g[1] + 1) * WIN],
                         o[:, 0:256].rearrange("p (c t) -> p c t", c=2))]
            if g[0] == "swa_sample":
                return [(lambda y, kv=kv, gg=gg: y[kv * HD:(kv + 1) * HD, 2 + gg, T_PROMPT:T].rearrange("p (b t) -> p b t", b=8),
                         o.rearrange("p (b kv g t) -> p b kv g t", b=8, kv=2, g=4)[kv * HD:(kv + 1) * HD, :, kv, gg, :])
                        for kv in range(2) for gg in range(4)]
            return [(lambda y, c=c, h=h: y[h * HD:(h + 1) * HD, 6 + c, T_PROMPT:T].rearrange("p (b t) -> p b t", b=8),
                     o.rearrange("p (c b h t) -> p c b h t", c=2, b=8, h=4)[h * HD:(h + 1) * HD, c, :, 2 * c + h, :])
                    for c in range(2) for h in range(2)]

        def first_key(group):
            return WIN if group[0] == "swa" and group[1] == 0 else 0

        @block.sync
        def _(sp):
            for s in range(2):
                sp.dma_start(mem[:, 4 * s:4 * s + 4, :], mem0[:, 4 * s:4 * s + 4, :]).then_inc(mem_in[s], 16)
                sp.dma_start(raw[:, s, :], wblk[s, :, :]).then_inc(raw_in[s], 16)
            def load_blocks(qq):
                for s in range(2):
                    b = sp.snap(qq * 2 + s)
                    src = wblk[bass.ds(b, 1), :, :].rearrange("o p n -> p (o n)")
                    sp.wait_ge(w_lo, b - 1)
                    sp.dma_start(raw[:, s, :], src).then_inc(raw_in[s], 16)

            load_blocks(1)
            sp.dma_start(cst[:, :], cst_d).then_inc(cst_in, 16)
            load_blocks(2)
            sp.dma_start(x[:, :, :], x0).then_inc(x_in, 16)
            with sp.Fori(3, PAIR_MEM + 1) as i:
                load_blocks(i)
            sp.wait_ge(pair_free[1], U_MEM + 1)
            sp.wait_ge(pair_free[0], U_MEM + 1)
            for l in range(L):
                sp.dma_start(mk_out[l], mtmp[:, l, 0:2 * N_MEM]).then_inc(mem_out, 16)
                sp.dma_start(mv_out[l], mtmp[:, l, 2 * N_MEM:]).then_inc(mem_out, 16)
            for l in range(L):
                sp.dma_start(kc_out[l], kcs_d[l].rearrange("p (b k) -> p b k", b=DEC_B)[:, :, DEC_T:WIN]).then_inc(stored, 16)
                sp.dma_start(vc_out[l], vcs_d[l, DEC_T:WIN, :]).then_inc(stored, 16)
            sp.wait_ge(mem_out, 64)
            with sp.Fori(0, L) as l:
                def lay(d):
                    return d[bass.ds(l, 1)].rearrange("o p n -> p (o n)")

                with sp.Fori(1, 12) as i:
                    load_blocks(pq(l, 0) + i)
                src = lay(par_d)
                sp.wait_ge(x_full, x_full_count(l, 0))
                sp.dma_start(par[:, :], src).then_inc(par_in, 16)
                with sp.Fori(12, 35) as i:
                    load_blocks(pq(l, 0) + i)
                srcs = [lay(d) for d in (kcs_d, vcs_d, mks_d, mk_out, mv_out)]
                sp.wait_ge(blk_done, pq(l, Q_IN) * 2)
                sp.dma_start(kcs[:, :, :].rearrange("p b k -> p (b k)"), srcs[0]).then_inc(caches_in, 16)
                sp.dma_start(vcs[:, :, :].rearrange("p b k -> p (b k)"), srcs[1]).then_inc(caches_in, 16)
                sp.dma_start(mcs[:, :, :].rearrange("p c k -> p (c k)"), srcs[2]).then_inc(caches_in, 16)
                sp.dma_start(mk[:, :, :].rearrange("p c k -> p (c k)"), srcs[3]).then_inc(memkv_in, 16)
                sp.dma_start(mv[:, :, :].rearrange("p c k -> p (c k)"), srcs[4]).then_inc(memkv_in, 16)
                with nc.allow_non_contiguous_dma(reason="15 columns per sequence"):
                    for c in range(2):
                        src = sps_d[bass.ds(l, 1), :, c, :, :].rearrange("o p b t -> p (o b) t")
                        sp.dma_start(xps[:, c, :, 0:POOL_STATE], src).then_inc(state_in, 16)
                with sp.Fori(35, 40) as i:
                    load_blocks(pq(l, 0) + i)
                src = lay(mvs_d)
                sp.wait_ge(scores_done, l * NG + 2)
                sp.dma_start(mcs[:, :, :].rearrange("p c k -> p (c k)"), src).then_inc(values_in, 16)
                with sp.Fori(40, 44) as i:
                    load_blocks(pq(l, 0) + i)
                dk = kT_out[bass.ds(l, 1)].rearrange("o p n -> p (o n)")
                dvp = v_out[bass.ds(l, 1), 0:P].rearrange("o p n -> p (o n)")
                dvs = v_out[bass.ds(l, 1), P:P + 64].rearrange("o p n -> p (o n)")
                dpp = [poolp_out[bass.ds(l, 1), :, c, :].rearrange("o p t -> p (o t)") for c in range(2)]
                dps = [pools_out[bass.ds(l, 1), :, c, :, :].rearrange("o p b t -> p (o b) t") for c in range(2)]
                sp.wait_ge(rope_done, l * 5 + 5)
                sp.dma_start(dk, k[:, 3 * WIN:T]).then_inc(stored, 16)
                sp.wait_ge(t_free, t_count(l, "v") + 2)
                sp.dma_start(dvp, v[:, 3, :]).then_inc(stored, 16)
                sp.dma_start(dvs, v[0:64, 4, :]).then_inc(stored, 16)
                sp.wait_ge(pair_free[0], n_use(l, U_IN + 4) + 2)
                sp.wait_ge(pair_free[1], n_use(l, U_IN + 4) + 2)
                sp.wait_ge(state_in, l * 32 + 32)
                with nc.allow_non_contiguous_dma(reason="15 columns per sequence"):
                    for c in range(2):
                        sp.dma_start(dpp[c], xpp[:, c, T_PROMPT:XP_P]).then_inc(stored, 16)
                        sp.dma_start(dps[c], xps[:, c, :, DEC_T:XP_S]).then_inc(stored, 16)
                with sp.Fori(44, PAIRS + 1) as i:
                    load_blocks(pq(l, 0) + i)
            for h in range(2):
                sp.wait_ge(x_full, x_full_count(L, 0) - (1 - h) * len(BY_DVE))
                sp.dma_start(y_out[:, :, half(h)], x[:, :, half(h)]).then_inc(final_out, 16)
            sp.wait_ge(final_out, 32)
            sp.wait_ge(stored, (4 + 7 * L) * 16)

        @block.scalar
        def _(act):
            act.sem_inc(pair_free[0], 1)
            act.sem_inc(pair_free[1], 1)
            act.sem_inc(s_free, 1)
            act.sem_inc(t_free, 1)
            act.sem_inc(x_full, 1)

            def round_w(qq, s, first=False):
                act.wait_ge(raw_in[s], (qq + 1) * 16)
                if not first:
                    act.wait_ge(blk_done, qq * 2 + s - 1)
                nc.scalar.activation(wh[:, s, :], raw[:, s, :], ACT.Copy).then_inc(w_hi, 1)

            act.wait_ge(small_set, 1)
            for s in range(2):
                act.wait_ge(mem_in[s], 16)
                cs = slice(4 * s, 4 * s + 4)
                nc.scalar.activation(memh[:, cs, :], mem[:, cs, :], ACT.Copy).then_inc(mem_hi, 1)
                round_w(0, s, first=True)
            for l in range(L):
                for what in range(2):
                    if (l, what) == (L - 1, 1):
                        act.wait_ge(x_in, 16)
                        for h in range(2):
                            for c in range(KC):
                                nc.scalar.activation(xh[:, c, half(h)], x[:, c, half(h)], ACT.Copy).then_inc(x_hi, 1)
                    for s in range(2):
                        act.wait_ge(blk_done, l * 4 + s + 1 if what == 0 else l * 4 + 4)
                        n = (2 * what + s) * N_MEM
                        nc.scalar.activation(mtmp[:, l, n:n + N_MEM], pair[s][:, 0, 0:N_MEM], ACT.Copy).then_inc(pair_free[s], 1)
                        round_w(l * 2 + (what + 1), s)

            def prime(function):
                nc.scalar.activation(small[:, 60:61], small[:, 61:62], function)

            def ffn(l, f):
                prime(ACT.Silu)
                with act.Fori(0, FC) as j:
                    qq = pq(l, Q_GU[f]) + j
                    u = n_use(l, U_GU[f]) + j
                    round_w(qq + 1, 0)
                    act.wait_ge(blk_done, qq * 2 + 1)
                    act.wait_ge(pair_free[1], u + 1)
                    nc.scalar.activation(two(tmp[:, 0, 0:T]), halves(pair[0]), ACT.Silu).then_inc(pair_free[0], 1)
                    round_w(qq + 1, 1)
                    act.wait_ge(pair_free[1], u + 2)
                    nc.scalar.activation(Hh[:, bass.ds(j * T, T)], tmp[:, 1, 0:T], ACT.Copy).then_inc(h_hi, 1)
                with act.Fori(0, 11) as i:
                    for s in range(2):
                        round_w(pq(l, Q_DOWN[f]) + i + 1, s)

            def layer_norm(l, n, nxt):
                prime(ACT.Sqrt)
                for h in range(2):
                    for c in range(KC):
                        act.wait_ge(cent, norm_count(l, n, h, c))
                        if h == 1 or c >= 4:
                            act.wait_ge(sq_used, norm_count(l, n, h, c - 4))
                        nc.scalar.activation(squares(h, c), x[:, c, half(h)], ACT.Square).then_inc(sq_ready, 1)
                        if h == 0 and c == 3:
                            round_w(nxt, 0)
                    if h == 0:
                        round_w(nxt, 1)
                    act.wait_ge(sq_used, norm_count(l, n, h, KC - 1))
                    nc.scalar.activation(tmp[:, 3, half(h)], S[:, h, 0:TH], ACT.Sqrt,
                                         bias=eps[:, 0:1]).then_inc((std_ready, s_free)[h], 1)
                for h in range(2):
                    for c in range(KC):
                        act.wait_ge(normed, norm_count(l, n, h, c))
                        b = par[:, P_LN + 16 * n + 8 + c:P_LN + 16 * n + 8 + c + 1]
                        last = nc.scalar.activation(xh[:, c, half(h)], x[:, c, half(h)], ACT.Identity, bias=b)
                        if c in BY_POOL:
                            act.drain()
                            last = nc.scalar.activation(x[:, c, half(h)], x[:, c, half(h)], ACT.Identity, bias=b)
                        last.then_inc(x_hi, 1)

            with act.Fori(0, L) as l:
                ffn(l, 0)
                act.wait_ge(par_in, l * 16 + 16)
                layer_norm(l, 0, pq(l, Q_IN))
                prime(ACT.Exp)

                def in_blk(off, s):
                    act.wait_ge(blk_done, pq(l, Q_IN + off) * 2 + s + 1)

                for i in range(5):
                    in_blk(i // 2, i % 2)
                    if i < 2:
                        round_w(pq(l, Q_IN + 1), i)
                    if i >= 2:
                        act.wait_ge(rope_done, l * 5 + i - 1)
                    nc.scalar.activation(two(tmp[:, i % 2, 0:T]), halves(pair[i % 2]), ACT.Copy,
                                         scale=HD ** -0.5 if i < 4 else 1.0).then_inc(pair_free[i % 2], 1)
                    if i >= 2:
                        round_w(pq(l, Q_IN + 1 + i // 2), i % 2)
                in_blk(2, 1)
                nc.scalar.activation(two(tmp[:, 2, 0:T]), halves(pair[1]), ACT.Copy).then_inc(pair_free[1], 1)
                round_w(pq(l, Q_IN + 3), 1)
                act.wait_ge(v_done, l + 1)
                nc.scalar.activation(v[:, 0:4, :], TP[:, 0, :].rearrange("p (s c) -> p s c", s=4), ACT.Copy)
                nc.scalar.activation(v[0:64, 4, :], TP[0:64, 1, 0:P], ACT.Copy).then_inc(t_free, 1)
                for c in range(2):
                    in_blk(3, c)
                    nc.scalar.activation(two(xq[:, c, :]), halves(pair[c]), ACT.Copy, scale=HD ** -0.5).then_inc(pair_free[c], 1)
                    round_w(pq(l, Q_IN + 4), c)

                def softmax_exp(i):
                    kind = GROUPS[i][0]
                    f = first_key(GROUPS[i])
                    act.wait_ge(max_ready, l * NG + i + 1)
                    src = score_view(S if kind in ("cross", "cross_sample") else prob[i % 2], kind)
                    dst = score_view(prob[i % 2], kind)
                    na = 1 if kind == "cross_sample" else 2
                    for j in range(2 * na):
                        last = nc.scalar.activation(dst[:, j // 2, j % 2, f:], src[:, j // 2, j % 2, f:], ACT.Exp,
                                                    bias=small[:, j:j + 1], accum_out=small[:, 8 + j:9 + j])
                    if kind in ("cross", "cross_sample"):
                        last.then_inc(s_free, 1)
                        act.drain().then_inc(exp_done, 1)
                    else:
                        nc.scalar.activation(small[:, 16:20], small[:, 4:8], ACT.Exp).then_inc(exp_done, 1)

                def copy_pt(i):
                    kind = GROUPS[i][0]
                    act.wait_ge(tr_done, l * NG + i + 1)
                    if kind == "swa_sample":
                        nc.scalar.activation(pt[:, 0:512], TP[:, 0, :], ACT.Copy)
                        nc.scalar.activation(pt[0:64, 512:1024], TP[0:64, 1, :], ACT.Copy).then_inc(t_free, 1)
                    elif kind == "cross_sample":
                        nc.scalar.activation(pt[:, 0:512], TP[:, 0, :], ACT.Copy).then_inc(t_free, 1)
                    elif first_key(GROUPS[i]):
                        nc.scalar.activation(pt[:, 512:1024], TP[:, 1, :], ACT.Copy).then_inc(t_free, 1)
                    else:
                        nc.scalar.activation(pt[:, :].rearrange("p (a n) -> p a n", a=2), TP[:, :, :], ACT.Copy).then_inc(t_free, 1)

                def out_hi(i):
                    act.wait_ge(pv_done, l * NG + i + 1)
                    for dst, src in out_parts(i):
                        last = nc.scalar.activation(dst(yh), src, ACT.Copy)
                    last.then_inc(y_hi, 1)

                def pool_hi(c):
                    act.wait_ge(mix_done, l * 2 + c + 1)
                    nc.scalar.activation(two(yh[:, c, :]), halves(S), ACT.Copy, scale=par[:, P_SCALE + c:P_SCALE + c + 1]).then_inc(y_hi, 1)

                softmax_exp(0)
                for i in range(NG):
                    copy_pt(i)
                    if i in (4, 5):
                        pool_hi(i - 4)
                    if i + 1 < NG:
                        softmax_exp(i + 1)
                    if i < 2:
                        in_blk(4, i)
                        nc.scalar.activation(xpp[:, i, POOL_STATE:POOL_STATE + TH], pair[i][:, 0, 0:TH], ACT.Copy)
                        nc.scalar.activation(xpp[:, i, POOL_STATE + TH:XP_P], pair[i][:, 1, 0:T_PROMPT - TH], ACT.Copy)
                        nc.scalar.activation(xps[:, i, :, POOL_STATE:XP_S],
                                             pair[i][:, 1, T_PROMPT - TH:TH].rearrange("p (b t) -> p b t", b=8),
                                             ACT.Copy).then_inc(pair_free[i], 1)
                        round_w(pq(l, Q_GATES), i)
                    else:
                        gi = i - 2
                        act.wait_ge(blk_done, pq(l, Q_GATES) * 2 + gi + 1)
                        nc.scalar.activation(two(gates[:, gi * T:(gi + 1) * T]), halves(pair[gi % 2]), ACT.Tanh,
                                             scale=0.5).then_inc(pair_free[gi % 2], 1)
                        round_w(pq(l, Q_GATES + 1 + gi // 2), gi % 2)
                    out_hi(i)

                act.wait_ge(stored, (4 + 7 * (l + 1)) * 16)
                with act.Fori(0, 2) as i:
                    for n, (what, mm) in enumerate(MERGE_STEPS):
                        qq = pq(l, Q_MERGE + n // 2) + i * 5
                        act.wait_ge(blk_done, qq * 2 + n % 2 + 1)
                        if what < 3:
                            m_old = i * 2 + (mm - 4)
                            act.wait_ge(merge_sum, l * 8 + i * 4 + (mm - 4) + 1)
                            nc.scalar.activation(two(gates[:, bass.ds((m_old * 3 + what) * T, T)]), halves(pair[n % 2]),
                                                 ACT.Tanh, scale=0.5).then_inc(pair_free[n % 2], 1)
                            round_w(qq + 1, n % 2)
                        else:
                            round_w(qq + 1, n % 2)
                            act.wait_ge(merge_sum, l * 8 + i * 4 + merge_order(mm) + 1)
                            m = i * 2 + mm
                            nc.scalar.activation(mgh[:, bass.ds(m * T, T)], tmp[:, merge_order(mm) % 2, 0:T],
                                                 ACT.Copy).then_inc(merge_hi, 1)
                with act.Fori(0, 3) as i:
                    for s in range(2):
                        round_w(pq(l, Q_WO) + i + 1, s)
                layer_norm(l, 1, pq(l, Q_GU[1]))
                ffn(l, 1)
                layer_norm(l, 2, pq(l, PAIRS))

        @block.vector
        def _(dve):
            def rest_w(qq, s):
                dve.wait_ge(w_hi, qq * 2 + s + 1)
                nc.vector.tensor_tensor(wl[:, s, :], raw[:, s, :], wh[:, s, :].bitcast(F32), ALU.subtract).then_inc(w_lo, 1)

            nc.vector.memset(eps[:, :], LN_EPS)
            nc.vector.memset(small[:, 60:62], 1.0).then_inc(small_set, 1)
            for s in range(2):
                cs = slice(4 * s, 4 * s + 4)
                dve.wait_ge(mem_hi, s + 1)
                nc.vector.tensor_tensor(meml[:, cs, :], mem[:, cs, :], memh[:, cs, :].bitcast(F32), ALU.subtract).then_inc(mem_ready, 1)
                rest_w(0, s)
            dve.wait_ge(cst_in, 16)
            with dve.Fori(1, PAIR_MEM) as i:
                for s in range(2):
                    rest_w(i, s)
            for h in range(2):
                for c in BY_DVE:
                    dve.wait_ge(x_hi, x_hi_count(0, 0, h, c))
                    nc.vector.tensor_tensor(xl[:, c, half(h)], x[:, c, half(h)], xh[:, c, half(h)].bitcast(F32),
                                            ALU.subtract).then_inc(x_lo, 1)
            for s in range(2):
                rest_w(PAIR_MEM, s)

            def add_residual(m, s, x_whole):
                xm = x[:, bass.ds(m, 1), :].rearrange("p o t -> p (o t)")
                dve.wait_ge(x_full, x_whole)
                nc.vector.scalar_tensor_tensor(out=two(xm), in0=two(xm), scalar=ALPHA, in1=halves(pair[s]),
                                               op0=ALU.mult, op1=ALU.add).then_inc(pair_free[s], 1)
                dve.drain()
                nc.vector.tensor_tensor(tmp[:, 2, 0:T], tmp[:, 2, 0:T], xm, ALU.add)
                dve.drain()

            def ffn(l, f):
                with dve.Fori(0, FC) as j:
                    qq = pq(l, Q_GU[f]) + j
                    u = n_use(l, U_GU[f]) + j
                    rest_w(qq + 1, 0)
                    dve.drain()
                    dve.wait_ge(blk_done, qq * 2 + 2)
                    dve.wait_ge(pair_free[0], u + 2)
                    nc.vector.scalar_tensor_tensor(out=two(tmp[:, 1, 0:T]), in0=two(tmp[:, 0, 0:T]), scalar=0.5,
                                                   in1=halves(pair[1]), op0=ALU.mult, op1=ALU.mult).then_inc(pair_free[1], 1)
                    rest_w(qq + 1, 1)
                    dve.wait_ge(h_hi, l * (2 * FC) + (f * FC + 1) + j)
                    hj = bass.ds(j * T, T)
                    nc.vector.tensor_tensor(Hl[:, hj], tmp[:, 1, 0:T], Hh[:, hj].bitcast(F32), ALU.subtract).then_inc(h_split, 1)
                nc.vector.memset(tmp[:, 2, 0:T], 0.0)
                dve.drain()

                def down(i, steps):
                    for n in steps:
                        qq = pq(l, Q_DOWN[f] + n // 2) + i * 3
                        rest_w(qq + 1, n % 2)
                        if n % 3 == 2:
                            dve.wait_ge(blk_done, qq * 2 + n % 2 + 1)
                            add_residual(i * 2 + n // 3, n // 3, x_full_count(l, 2 * f))

                with dve.Fori(0, 3) as i:
                    down(i, range(6))
                down(3, range(4))

            def layer_norm(l, n, nxt, tail):
                def residual(h):
                    for m, s in tail:
                        xm = x[:, m, half(h)]
                        last = nc.vector.scalar_tensor_tensor(out=xm, in0=xm, scalar=ALPHA, in1=pair[s][:, h, 0:TH],
                                                              op0=ALU.mult, op1=ALU.add)
                        if h == 1:
                            last.then_inc(pair_free[s], 1)
                        dve.drain()
                        nc.vector.tensor_tensor(tmp[:, 2, half(h)], tmp[:, 2, half(h)], xm, ALU.add)
                    dve.drain().then_inc(sum_ready, 1)

                def center(h):
                    dve.wait_ge(mean_done, l * 6 + (2 * n + h + 1))
                    for c in range(KC):
                        nc.vector.tensor_tensor(x[:, c, half(h)], x[:, c, half(h)], TP[:, h, 0:TH], ALU.subtract).then_inc(cent, 1)

                def scale(h):
                    nc.vector.reciprocal(tmp[:, 3, half(h)], tmp[:, 3, half(h)])
                    dve.drain()
                    for c in range(KC + 1):
                        if c < KC:
                            g = par[:, P_LN + 16 * n + c:P_LN + 16 * n + c + 1]
                            xc = x[:, c, half(h)]
                            nc.vector.scalar_tensor_tensor(out=xc, in0=xc, scalar=g, in1=tmp[:, 3, half(h)],
                                                           op0=ALU.mult, op1=ALU.mult).then_inc(normed, 1)
                        if c - 1 in BY_DVE:
                            b = par[:, P_LN + 16 * n + 8 + c - 1:P_LN + 16 * n + 8 + c]
                            dve.wait_ge(x_hi, x_hi_count(l, n + 1, h, c - 1))
                            nc.vector.scalar_tensor_tensor(out=xl[:, c - 1, half(h)], in0=x[:, c - 1, half(h)], scalar=b,
                                                           in1=xh[:, c - 1, half(h)].bitcast(F32), op0=ALU.add,
                                                           op1=ALU.subtract).then_inc(x_lo, 1)

                dve.wait_ge(half_done, l * 3 + (n + 1))
                residual(0)
                center(0)
                rest_w(nxt, 0)
                dve.wait_ge(blk_done, nxt * 2)
                residual(1)
                center(1)
                dve.drain().then_inc(t_free, 1)
                rest_w(nxt, 1)
                dve.wait_ge(std_ready, l * 3 + (n + 1))
                scale(0)
                dve.wait_ge(s_free, s_count(l, f"var{n}") + 2)
                scale(1)

            with dve.Fori(0, L) as l:
                ffn(l, 0)
                dve.wait_ge(par_in, l * 16 + 16)
                layer_norm(l, 0, pq(l, Q_IN), [(7, 1)])
                nc.vector.tensor_scalar(par[:, P_SCALE:P_SCALE + 2], par[:, P_SCALE:P_SCALE + 2], 0.5, None, ALU.mult)
                nc.vector.tensor_scalar(small[:, 32:41], par[:, P_SINK:P_SINK + 9], -1.0, None, ALU.mult)

                nc.vector.memset(xpp[:, :, 0:POOL_STATE], 0.0)
                nc.vector.memset(qbd, 0.0)
                nc.vector.memset(xbd, 0.0)

                def rope(i):
                    dst = q[:, i, :] if i < 4 else k[:, :]
                    dve.drain()
                    dve.wait_ge(rot_done, l * 5 + i + 1)
                    nc.vector.tensor_tensor(dst, tmp[:, i % 2, 0:T], cst[:, C_COS:C_COS + T], ALU.mult)
                    nc.vector.tensor_tensor(two(prob[0][:, 0:T]), two(cst[:, C_SIN:C_SIN + T]), halves(S), ALU.mult).then_inc(s_free, 1)
                    dve.drain()
                    nc.vector.tensor_tensor(dst, dst, prob[0][:, 0:T], ALU.add).then_inc(rope_done, 1)

                for i in range(5):
                    rest_w(pq(l, Q_IN + 1 + i // 2), i % 2)
                    if i > 0:
                        rope(i - 1)
                rest_w(pq(l, Q_IN + 3), 1)
                rope(4)
                for kv in range(2):
                    a = kv * HD
                    for g in range(4):
                        last = nc.vector.tensor_copy(qbd[a:a + HD, :, kv * 32 + g * 8:kv * 32 + g * 8 + 8],
                                                     q[a:a + HD, g, T_PROMPT:T].rearrange("p (b t) -> p b t", b=8))
                last.then_inc(qbd_ready, 1)
                rest_w(pq(l, Q_IN + 4), 0)
                for c in range(2):
                    dve.wait_ge(pair_free[c], n_use(l, U_IN + 3) + 2)
                    for h in range(2):
                        a = h * HD
                        last = nc.vector.tensor_copy(xbd[a:a + HD, c, :, (2 * c + h) * 8:(2 * c + h) * 8 + 8],
                                                     xq[a:a + HD, c, T_PROMPT:T].rearrange("p (b t) -> p b t", b=8))
                last.then_inc(xbd_ready, 1)

                def softmax_max(i):
                    kind = GROUPS[i][0]
                    f = first_key(GROUPS[i])
                    dve.wait_ge(scores_done, l * NG + i + 1)
                    s4, p4 = score_view(S, kind), score_view(prob[i % 2], kind)
                    if kind == "swa":
                        for a in range(2):
                            m = cst[:, C_MASK + f:C_MASK + 2 * P].unsqueeze(1).to_broadcast([P, 2, 2 * P - f])
                            last = nc.vector.tensor_tensor(p4[:, a, :, f:], s4[:, a, :, f:], m, ALU.add)
                        last.then_inc(s_free, 1)
                    elif kind == "swa_sample":
                        for a in range(2):
                            m = cst[:, C_MSC:C_MSC + P].unsqueeze(1).to_broadcast([P, 2, P])
                            nc.vector.tensor_tensor(p4[:, a, :, 0:P], s4[:, a, :, 0:P], m, ALU.add)
                            m = cst[:, C_MSN + a * 128:C_MSN + a * 128 + 128].rearrange("p (b k) -> p b k", b=2)
                            last = nc.vector.tensor_tensor(p4[:, a, :, P:192], s4[:, a, :, P:192], m, ALU.add)
                        last.then_inc(s_free, 1)
                    masked = kind in ("swa", "swa_sample")
                    if masked:
                        dve.drain()
                    src = p4 if masked else s4
                    nj = 2 if kind == "cross_sample" else 4
                    last = nc.vector.tensor_reduce(small[:, 0:nj].rearrange("p (a b) -> p a b", b=2), src[:, :, :, f:],
                                                   AX.X, ALU.max, negate=True)
                    if masked:
                        dve.drain()
                        if kind == "swa":
                            kv = GROUPS[i][2]
                            nc.vector.tensor_tensor(small[:, 0:4], small[:, 0:4], small[:, 32 + 4 * kv:36 + 4 * kv], ALU.min)
                            dve.drain()
                            last = nc.vector.tensor_tensor(small[:, 4:8], small[:, 0:4],
                                                           par[:, P_SINK + 4 * kv:P_SINK + 4 * kv + 4], ALU.add)
                        else:
                            nc.vector.tensor_scalar(small[:, 0:4], small[:, 0:4], small[:, 40:41], None, ALU.min)
                            dve.drain()
                            last = nc.vector.tensor_scalar(small[:, 4:8], small[:, 0:4], par[:, P_SROW:P_SROW + 1], None, ALU.add)
                    last.then_inc(max_ready, 1)

                def softmax_div(i):
                    kind = GROUPS[i][0]
                    f = first_key(GROUPS[i])
                    nj = 2 if kind == "cross_sample" else 4
                    dve.wait_ge(exp_done, l * NG + i + 1)
                    if kind in ("swa", "swa_sample"):
                        nc.vector.tensor_tensor(small[:, 8:12], small[:, 8:12], small[:, 16:20], ALU.add)
                        dve.drain()
                    nc.vector.reciprocal(small[:, 20:20 + nj], small[:, 8:8 + nj])
                    dve.drain()
                    p4 = score_view(prob[i % 2], kind)
                    for j in range(nj):
                        pj = p4[:, j // 2, j % 2, f:]
                        last = nc.vector.tensor_scalar(pj, pj, small[:, 20 + j:21 + j], 0.5, ALU.mult, ALU.mult)
                    last.then_inc(prob_ready, 1)

                def y_before(i):
                    return l * (NG + 2) + i + max(0, min(2, i - 3))

                def out_lo(i):
                    dve.wait_ge(y_hi, y_before(i) + 1)
                    for dst, src in out_parts(i):
                        last = nc.vector.tensor_tensor(dst(yl), src, dst(yh).bitcast(F32), ALU.subtract)
                    last.then_inc(t_free, 1)

                def pool_lo(c):
                    dve.wait_ge(y_hi, l * (NG + 2) + 4 + 2 * c + 1)
                    nc.vector.scalar_tensor_tensor(out=two(yl[:, c, :]), in0=halves(S), scalar=par[:, P_SCALE + c:P_SCALE + c + 1],
                                                   in1=two(yh[:, c, :]).bitcast(F32), op0=ALU.mult, op1=ALU.subtract).then_inc(s_free, 1)

                softmax_max(0)
                rest_w(pq(l, Q_IN + 4), 1)
                softmax_div(0)
                for i in range(NG):
                    if i + 1 < NG:
                        softmax_max(i + 1)
                    if i in (4, 5):
                        pool_lo(i - 4)
                    if i + 1 < NG:
                        softmax_div(i + 1)
                    out_lo(i)
                    rest_w(pq(l, Q_GATES + i // 2), i % 2)

                with dve.Fori(0, 2) as i:
                    for n, (what, mm) in enumerate(MERGE_STEPS):
                        qq = pq(l, Q_MERGE + n // 2) + i * 5
                        rest_w(qq + 1, n % 2)
                        if what == 3:
                            o = merge_order(mm)
                            m = i * 2 + mm
                            gslot = (i * 2 + mm % 4) * 3
                            acc = tmp[:, o % 2, 0:T]
                            dve.wait_ge(blk_done, qq * 2 + n % 2 + 1)
                            if mm >= 4:
                                for s in range(2):
                                    n_gate = max(k for k in range(s, n, 2) if MERGE_STEPS[k][1] == mm)
                                    dve.wait_ge(pair_free[s], n_use(l, U_MERGE + n_gate // 2) + i * 5 + 2)
                            part = (acc, tmp[:, 2, 0:T], tmp[:, 3, 0:T])
                            sources = [(2, pair[n % 2], pair_free[n % 2]), (0, S, s_free), (1, TP, t_free)]
                            if n == len(MERGE_STEPS) - 1:
                                sources[0:2] = sources[1::-1]
                            for (b, ps, freed), out in zip(sources, part):
                                g = gates[:, bass.ds((gslot + b) * T, T)]
                                nc.vector.scalar_tensor_tensor(out=two(out), in0=two(g), scalar=1.0, in1=halves(ps),
                                                               op0=ALU.add, op1=ALU.mult).then_inc(freed, 1)
                            dve.drain()
                            nc.vector.tensor_tensor(acc, acc, part[1], ALU.add)
                            dve.drain()
                            nc.vector.tensor_tensor(acc, acc, part[2], ALU.add).then_inc(merge_sum, 1)
                            dve.wait_ge(merge_hi, l * 8 + i * 4 + o + 1)
                            mt = bass.ds(m * T, T)
                            nc.vector.tensor_tensor(mgl[:, mt], acc, mgh[:, mt].bitcast(F32), ALU.subtract).then_inc(merge_ready, 1)
                nc.vector.memset(tmp[:, 2, 0:T], 0.0)
                dve.drain()
                with dve.Fori(0, 3) as i:
                    for s in range(2):
                        qq = pq(l, Q_WO) + i
                        rest_w(qq + 1, s)
                        dve.wait_ge(blk_done, qq * 2 + s + 1)
                        add_residual(i * 2 + s, s, x_full_count(l, 1))
                layer_norm(l, 1, pq(l, Q_GU[1]), [(6, 0), (7, 1)])
                ffn(l, 1)
                layer_norm(l, 2, pq(l, PAIRS), [(7, 1)])

        @block.gpsimd
        def _(pool):
            def finish_norm(l, n):
                for h in range(2):
                    for c in BY_POOL:
                        pool.wait_ge(x_hi, x_hi_count(l, n + 1, h, c))
                        nc.gpsimd.tensor_tensor(xl[:, c, half(h)], x[:, c, half(h)], xh[:, c, half(h)].bitcast(F32),
                                                ALU.subtract).then_inc(x_lo_p, 1)
                for h in range(2):
                    for c in BY_DVE:
                        b = par[:, P_LN + 16 * n + 8 + c:P_LN + 16 * n + 8 + c + 1]
                        pool.wait_ge(*x_split(l, n + 1, h, c))
                        nc.gpsimd.tensor_tensor(x[:, c, half(h)], x[:, c, half(h)], b.to_broadcast([P, TH]),
                                                ALU.add).then_inc(x_full, 1)

            def windows(c, t0, t1):
                def view(t):
                    return (tmp[:, t, 0:XP_P].unsqueeze(1),
                            tmp[:, t, XP_P:TMP].rearrange("p (b t) -> p b t", b=DEC_B))
                src = (xpp[:, c, :].unsqueeze(1), xps[:, c, :, :])
                w, reach = 1, 0
                out = []
                bufs = [view(t0), view(t1)]
                for step in range(2 if c == 0 else 4):
                    dst = bufs[step % 2]
                    reach += w
                    for d, s in zip(dst, src):
                        n = s.shape[-1]
                        nc.gpsimd.tensor_tensor(d[:, :, reach:n], s[:, :, reach:n], s[:, :, reach - w:n - w], ALU.add)
                    pool.drain()
                    w *= 2
                    src = dst
                return bufs

            for h in range(2):
                for c in BY_POOL:
                    pool.wait_ge(x_hi, x_hi_count(0, 0, h, c))
                    nc.gpsimd.tensor_tensor(xl[:, c, half(h)], x[:, c, half(h)], xh[:, c, half(h)].bitcast(F32),
                                            ALU.subtract).then_inc(x_lo_p, 1)
            pool.wait_ge(cst_in, 16)
            with pool.Fori(0, L) as l:
                pool.wait_ge(par_in, l * 16 + 16)
                finish_norm(l, 0)
                pool.wait_ge(rope_done, l * 5 + 5)
                pool.wait_ge(state_in, l * 32 + 32)
                for c in range(2):
                    pool.wait_ge(pair_free[c], n_use(l, U_IN + 4) + 2)
                    bufs = windows(c, 2, 3)
                    dp = tmp[:, c, 0:T_PROMPT]
                    ds_ = tmp[:, c, T_PROMPT:T].rearrange("p (b t) -> p b t", b=DEC_B)
                    for h in range(2):
                        a = slice(h * 64, h * 64 + 64)
                        iv = cst[a, C_INVW + c:C_INVW + c + 1]
                        wp, ws = bufs[h]
                        nc.gpsimd.tensor_scalar(dp[a, :], wp[a, 0, POOL_STATE:XP_P], iv, 0.0, ALU.mult, ALU.add)
                        nc.gpsimd.tensor_scalar(ds_[a], ws[a, :, POOL_STATE:XP_S], iv, 0.0, ALU.mult, ALU.add)
                    pool.drain()
                    for h in range(2):
                        a = slice(h * 64, h * 64 + 64)
                        wp, _ = bufs[h]
                        nc.gpsimd.tensor_tensor(dp[a, 0:16], wp[a, 0, POOL_STATE:POOL_STATE + 16],
                                                cst[a, C_TAB + 16 * c:C_TAB + 16 * c + 16], ALU.mult)
                    pool.drain()
                    nc.gpsimd.tensor_tensor(dp, dp, xpp[:, c, POOL_STATE:XP_P], ALU.subtract)
                    nc.gpsimd.tensor_tensor(ds_, ds_, xps[:, c, :, POOL_STATE:XP_S], ALU.subtract)
                    pool.drain().then_inc(diff_ready, 1)
                finish_norm(l, 1)
                finish_norm(l, 2)

        @block.tensor
        def _(pe):
            def mm3(out, wt, xt, kk, nk, halves=(0, 1)):
                for h in halves:
                    nc.tensor.matmul(out(h), wt[0], xt[0](h), start=(kk == 0), stop=False)
                for h in halves:
                    nc.tensor.matmul(out(h), wt[0], xt[1](h), start=False, stop=False)
                for h in halves:
                    last = nc.tensor.matmul(out(h), wt[1], xt[0](h), start=False, stop=(kk == nk - 1))
                return last

            def wt(s, c):
                return wh[:, s, c * P:(c + 1) * P], wl[:, s, c * P:(c + 1) * P]

            def two_halves(ap):
                return ap.rearrange("p (s f) -> p s f", s=2)

            def xs(t, c):
                return lambda h: t[:, c, h * TH:(h + 1) * TH]

            def begin(qq, s, u=None):
                pe.wait_ge(w_lo, qq * 2 + s + 1)
                if u is not None:
                    pe.wait_ge(pair_free[s], u + 1)

            def project(l, qq, s, u, halfway=None):
                begin(qq, s, u)
                for c in range(KC):
                    if c == KC // 2 and halfway:
                        halfway()
                    last = mm3(lambda h: pair[s][:, h, 0:TH], wt(s, c), (xs(xh, c), xs(xl, c)), c, KC)
                last.then_inc(blk_done, 1)

            def project_first(l, n, qq, u):
                begin(qq, 0, u)
                begin(qq, 1, u)
                lag = KC // 2
                turns = [(0, c, s) for c in range(KC) for s in range(2)]
                turns += [(1, c, 0) for c in range(lag)]
                turns += [(1, c - lag * s, s) for c in range(lag, KC) for s in range(2)]
                turns += [(1, c, 1) for c in range(KC - lag, KC)]
                for h, c, s in turns:
                    if s == 0:
                        pe.wait_ge(*x_split(l, n, h, c))
                    last = mm3(lambda h: pair[s][:, h, 0:TH], wt(s, c), (xs(xh, c), xs(xl, c)), c, KC, (h,))
                    if h == 1 and c == KC - 1:
                        last.then_inc(blk_done, 1)

            with pe.Fori(0, L) as l:
                for s in range(2):
                    begin(l * 2, s, l * 2)
                    for c in range(KC):
                        pe.wait_ge(mem_ready, c // 4 + 1)
                        last = mm3(lambda h: pair[s][:, 0, 0:N_MEM], wt(s, c),
                                   (lambda h: memh[:, c, :], lambda h: meml[:, c, :]), c, KC, (0,))
                    last.then_inc(blk_done, 1)
                for s in range(2):
                    begin(l * 2 + 1, s, l * 2 + 1)
                for j in range(2):
                    js = slice(j * P, (j + 1) * P)
                    for c in range(KC):
                        both = [lambda h, w=w: w[:, :, c * P:(c + 1) * P] for w in (wh, wl)]
                        last = mm3(lambda h: two_halves(pair[j][:, 0, 0:2 * P]), (memh[:, c, js], meml[:, c, js]),
                                   both, c, KC, (0,))
                last.then_inc(blk_done, 2)

            def mean(l, n, h):
                pe.wait_ge(sum_ready, l * 6 + (2 * n + h + 1))
                if h == 0:
                    pe.wait_ge(t_free, t_count(l, f"mean{n}") + 1)
                nc.tensor.matmul(TP[:, h, 0:TH], ones, tmp[:, 2, half(h)], start=True, stop=True).then_inc(mean_done, 1)

            def variance(l, n, h):
                if h == 0:
                    pe.wait_ge(s_free, s_count(l, f"var{n}") + 1)
                for c in range(KC):
                    pe.wait_ge(sq_ready, norm_count(l, n, h, c))
                    nc.tensor.matmul(S[:, h, 0:TH], ones, squares(h, c), start=(c == 0),
                                     stop=(c == KC - 1)).then_inc(sq_used, 1)

            def finish_halves(l, n, qq, parts):
                for h in range(2):
                    for s, (p, tiles, moving, k0, nk, u) in enumerate(parts):
                        if h == 0:
                            begin(qq, s, u)
                        for c in range(tiles):
                            last = mm3(lambda h: pair[p][:, h, 0:TH], wt(s, c), moving(k0 + c), k0 + c, nk, (h,))
                            if h == 1 and s == 0 and c == 4:
                                mean(l, n, 0)
                        if h == 1:
                            last.then_inc(blk_done, 1)
                        elif s == 1:
                            last.then_inc(half_done, 1)
                variance(l, n, 0)
                mean(l, n, 1)
                variance(l, n, 1)

            def ffn(l, f):
                project_first(l, 2 * f, pq(l, Q_GU[f]), n_use(l, U_GU[f]))
                with pe.Fori(1, FC) as j:
                    for s in range(2):
                        project(l, pq(l, Q_GU[f]) + j, s, n_use(l, U_GU[f]) + j)

                def hidden(kk):
                    return [lambda h, t=t: t[:, kk * T + h * TH:kk * T + (h + 1) * TH] for t in (Hh, Hl)]

                def down(i, m, blocks):
                    for n in blocks:
                        nb = 3 * m + n
                        qq = pq(l, Q_DOWN[f] + nb // 2) + i * 3
                        begin(qq, nb % 2)
                        pe.wait_ge(h_split, l * (2 * FC) + (f * FC + min(8 * n + 8, FC)))
                        if n == 0:
                            pe.wait_ge(pair_free[m], n_use(l, U_DOWN[f]) + i + 1)
                        for c in range(8 if n < 2 else 6):
                            kk = 8 * n + c
                            last = mm3(lambda h: pair[m][:, h, 0:TH], wt(nb % 2, c), hidden(kk), kk, FC)
                        last.then_inc(blk_done, 1)

                with pe.Fori(0, 3) as i:
                    for m in range(2):
                        down(i, m, range(3))
                down(3, 0, range(3))
                down(3, 1, range(1))
                finish_halves(l, 2 * f, pq(l, Q_DOWN[f] + 11),
                              [(1, 8, hidden, 8, FC, None), (1, 6, hidden, 16, FC, None)])

            pe.wait_ge(cst_in, 16)
            with pe.Fori(0, L) as l:
                ffn(l, 0)

                def rotate(i):
                    pe.wait_ge(pair_free[i % 2], n_use(l, U_IN + i // 2) + 2)
                    pe.wait_ge(s_free, s_count(l, ("rot", i)) + 1)
                    for h in range(2):
                        last = nc.tensor.matmul(S[:, h, 0:TH], rot, tmp[:, i % 2, h * TH:(h + 1) * TH], start=True, stop=True)
                    last.then_inc(rot_done, 1)

                def scores(i):
                    g = GROUPS[i]
                    pe.wait_ge(s_free, s_count(l, ("scores", i)) + 1)
                    s4 = score_view(S, g[0])
                    if g[0] == "swa":
                        _, n, kv = g
                        a = slice(kv * HD, kv * HD + HD)
                        f = first_key(g)
                        for j in range(4):
                            last = nc.tensor.matmul(s4[:, j // 2, j % 2, f:], q[a, j, n * WIN:(n + 1) * WIN],
                                                    k[a, (n - 1) * WIN + f:(n + 1) * WIN], start=True, stop=True)
                    elif g[0] == "cross":
                        pe.wait_ge(memkv_in, l * 32 + 32)
                        for j in range(4):
                            a = slice((j // 2) * HD, (j // 2) * HD + HD)
                            last = nc.tensor.matmul(s4[:, j // 2, j % 2, :], xq[a, j % 2, g[1] * WIN:(g[1] + 1) * WIN],
                                                    mk[a, j % 2, :], start=True, stop=True)
                    elif g[0] == "swa_sample":
                        pe.wait_ge(qbd_ready, l + 1)
                        pe.wait_ge(caches_in, l * 48 + 48)
                        for b in range(DEC_B):
                            t, r = b // 2, (b % 2) * 64
                            o = s4[r:r + 64, t // 2, t % 2, :]
                            nc.tensor.matmul(o[:, 0:P], qbd[:, b, :], kcs[:, b, :], start=True, stop=True)
                            last = nc.tensor.matmul(o[:, P:192], qbd[:, b, :], k[:, T_PROMPT:T], start=True, stop=True)
                    else:
                        pe.wait_ge(xbd_ready, l + 1)
                        for b in range(DEC_B):
                            t, r = b // 4, (b % 4) * 32
                            for c in range(2):
                                last = nc.tensor.matmul(s4[r:r + 32, 0, t, :], xbd[:, c, b, :],
                                                        mcs[:, c, b * N_MEM:(b + 1) * N_MEM], start=(c == 0), stop=(c == 1),
                                                        tile_position=(0, r))
                    last.then_inc(scores_done, 1)

                def transposes(i):
                    g = GROUPS[i]
                    pe.wait_ge(prob_ready, l * NG + i + 1)
                    pe.wait_ge(t_free, t_count(l, ("tr", i)) + 1)
                    p4 = score_view(prob[i % 2], g[0])
                    if g[0] == "swa_sample":
                        for t in range(4):
                            cols = slice(t * P, (t + 1) * P)
                            nc.tensor.transpose(TP[:, 0, cols], p4[:, t // 2, t % 2, 0:P], ident)
                            last = nc.tensor.transpose(TP[0:64, 1, cols], p4[:, t // 2, t % 2, P:192], ident)
                    elif g[0] == "cross_sample":
                        for t in range(2):
                            for kc in range(2):
                                cols = slice((t * 2 + kc) * P, (t * 2 + kc + 1) * P)
                                last = nc.tensor.transpose(TP[:, 0, cols], p4[:, 0, t, kc * P:(kc + 1) * P], ident)
                    else:
                        for kc in range(first_key(g) // P, 2):
                            for j in range(4):
                                last = nc.tensor.transpose(TP[:, kc, j * P:(j + 1) * P],
                                                           p4[:, j // 2, j % 2, kc * P:(kc + 1) * P], ident)
                    last.then_inc(tr_done, 1)

                def values(i):
                    g = GROUPS[i]
                    pe.wait_ge(t_free, t_count(l, ("pv", i)) + 1)
                    o = TP[:, 0, :]
                    if g[0] == "swa":
                        _, n, kv = g
                        a = slice(kv * HD, kv * HD + HD)
                        k0 = first_key(g) // P
                        for j in range(4):
                            for kc in range(k0, 2):
                                last = nc.tensor.matmul(o[a, j * P:(j + 1) * P], v[:, n - 1 + kc, a],
                                                        pt[:, kc * 512 + j * P:kc * 512 + (j + 1) * P],
                                                        start=(kc == k0), stop=(kc == 1))
                    elif g[0] == "cross":
                        for j in range(4):
                            a = slice((j // 2) * HD, (j // 2) * HD + HD)
                            head = 2 * (j % 2) + j // 2
                            for kc in range(2):
                                last = nc.tensor.matmul(o[a, (j % 2) * P:(j % 2 + 1) * P], mv[:, kc, head * HD:(head + 1) * HD],
                                                        pt[:, kc * 512 + j * P:kc * 512 + (j + 1) * P],
                                                        start=(kc == 0), stop=(kc == 1))
                    elif g[0] == "swa_sample":
                        for b in range(DEC_B):
                            cols = slice(b * 64, (b + 1) * 64)
                            nc.tensor.matmul(o[:, cols], vcs[:, b, :], pt[:, cols], start=True, stop=False)
                            last = nc.tensor.matmul(o[:, cols], v[0:64, 4, :], pt[0:64, 512 + b * 64:512 + (b + 1) * 64],
                                                    start=False, stop=True)
                    else:
                        pe.wait_ge(values_in, l * 16 + 16)
                        for b in range(DEC_B):
                            for c in range(2):
                                for kc in range(2):
                                    col = ((b // 4) * 2 + kc) * P + (b % 4) * 32
                                    last = nc.tensor.matmul(o[:, (c * 8 + b) * 32:(c * 8 + b + 1) * 32],
                                                            mcs[:, kc, b * N_MEM + c * P:b * N_MEM + (c + 1) * P],
                                                            pt[:, col:col + 32], start=(kc == 0), stop=(kc == 1))
                    last.then_inc(pv_done, 1)

                def mix(c):
                    pe.wait_ge(par_in, l * 16 + 16)
                    pe.wait_ge(diff_ready, l * 2 + c + 1)
                    pe.wait_ge(s_free, s_count(l, ("mix", c)) + 1)
                    for h in range(2):
                        last = nc.tensor.matmul(S[:, h, 0:TH], par[:, P_MIX + c * P:P_MIX + (c + 1) * P],
                                                tmp[:, c, h * TH:(h + 1) * TH], start=True, stop=True)
                    last.then_inc(mix_done, 1)

                project_first(l, 1, pq(l, Q_IN), n_use(l, U_IN))
                for i in range(2, 5):
                    project(l, pq(l, Q_IN + i // 2), i % 2, n_use(l, U_IN + i // 2))
                    rotate(i - 2)
                project(l, pq(l, Q_IN + 2), 1, n_use(l, U_IN + 2))
                rotate(3)
                pe.wait_ge(pair_free[1], n_use(l, U_IN + 2) + 2)
                pe.wait_ge(t_free, t_count(l, "v") + 1)
                for t in range(4):
                    nc.tensor.transpose(TP[:, 0, t * P:(t + 1) * P], tmp[:, 2, t * P:(t + 1) * P], ident)
                nc.tensor.transpose(TP[0:64, 1, 0:P], tmp[:, 2, T_PROMPT:T], ident).then_inc(v_done, 1)
                project(l, pq(l, Q_IN + 3), 0, n_use(l, U_IN + 3))
                rotate(4)
                project(l, pq(l, Q_IN + 3), 1, n_use(l, U_IN + 3))
                scores(0)
                for i in range(NG):
                    if 0 < i < NG - 1:
                        scores(i + 1)

                    def between():
                        if i == 0:
                            scores(1)
                        transposes(i)
                        if i in (4, 5):
                            mix(i - 4)

                    if i < 2:
                        project(l, pq(l, Q_IN + 4), i, n_use(l, U_IN + 4), between)
                    else:
                        project(l, pq(l, Q_GATES + (i - 2) // 2), i % 2, n_use(l, U_GATES + (i - 2) // 2), between)
                    values(i)
                with pe.Fori(0, 2) as i:
                    for n, (what, mm) in enumerate(MERGE_STEPS):
                        s = n % 2
                        qq = pq(l, Q_MERGE + n // 2) + i * 5
                        u = n_use(l, U_MERGE + n // 2) + i * 5
                        if what < 3:
                            project(l, qq, s, u)
                            continue
                        begin(qq, s, u)
                        o = merge_order(mm)
                        cross, pool, swa = (pair[s], (6, 7)), (S, (0, 1)), (TP, (2, 3, 4, 5))
                        for dst, tiles in (pool, cross, swa) if n == 0 else (cross, pool, swa):
                            if n == 0 and dst is pair[s]:
                                pe.wait_ge(t_free, t_count(l, ("pv", NG - 1)) + 2)
                            if dst is S:
                                pe.wait_ge(s_free, l * NS + (S_USE[("merge", o)] + 1) + i * 4)
                            if dst is TP:
                                pe.wait_ge(t_free, l * NT + (T_USE[("merge", o)] + 1) + i * 4)
                            for j, c in enumerate(tiles):
                                last = mm3(lambda h: dst[:, h, 0:TH], wt(s, c), (xs(yh, c), xs(yl, c)), j, len(tiles))
                        last.then_inc(blk_done, 1)

                def merged(c):
                    return [lambda h, t=t: t[:, c * T + h * TH:c * T + (h + 1) * TH] for t in (mgh, mgl)]

                turns = [(s, part * 4 + n) for part in range(2) for s in range(2) for n in range(4)]
                for s, n in turns:
                    if n == 0:
                        begin(pq(l, Q_WO), s, n_use(l, U_WO))
                    if s == 0:
                        pe.wait_ge(merge_ready, l * 8 + n + 1)
                    last = mm3(lambda h: pair[s][:, h, 0:TH], wt(s, MERGED[n]), merged(MERGED[n]), n, KC)
                    if n == KC - 1:
                        last.then_inc(blk_done, 1)
                with pe.Fori(1, 3) as i:
                    for s in range(2):
                        begin(pq(l, Q_WO) + i, s, n_use(l, U_WO) + i)
                        for c in range(KC):
                            last = mm3(lambda h: pair[s][:, h, 0:TH], wt(s, c), merged(c), c, KC)
                        last.then_inc(blk_done, 1)
                finish_halves(l, 1, pq(l, Q_WO + 3),
                              [(s, KC, merged, 0, KC, n_use(l, U_WO + 3)) for s in range(2)])
                ffn(l, 1)


def _tiles(w, cols, np):
    return w[:, cols].reshape(-1, P, P).transpose(1, 0, 2).reshape(P, -1)


def pack_weights(a, np):
    perm = np.array([(kv * 4 + g) * HD + d for g in range(4) for kv in range(2) for d in range(HD)])
    blocks = []
    for l in range(L):
        for w in (a["w_mem_k"][l], a["w_mem_v"][l]):
            blocks += [_tiles(w, slice(c * P, (c + 1) * P), np) for c in range(2)]
    pad = np.zeros((2 * P, P), np.float32)
    for l in range(L):
        def ffn(name):
            out = []
            for j in range(FC):
                for w in (a[name + "_w_gate"][l], a[name + "_w_up"][l]):
                    out.append(_tiles(w, slice(j * P, (j + 1) * P), np))
            for m in range(KC):
                w = np.concatenate([a[name + "_w_down"][l][:, m * P:(m + 1) * P], pad])
                out += [_tiles(w[n * 8 * P:(n + 1) * 8 * P], slice(0, P), np) for n in range(3)]
            return out
        blocks += ffn("ffn1")
        w = a["w_in"][l]
        pool, swq, k, v, xq, gate = np.split(w, [256, 768, 896, 1024, 1280], axis=1)
        early = [gate[:, b * D + m * P:b * D + (m + 1) * P] for m in range(4) for b in range(3)]
        for w in [swq[:, perm], k, v, xq, pool] + early:
            blocks += [_tiles(w, slice(c * P, (c + 1) * P), np) for c in range(w.shape[1] // P)]
        br = np.concatenate([a["w_br_pool"][l], a["w_br_swa"][l][perm], a["w_br_cross"][l]])
        for i in range(2):
            for what, mm in MERGE_STEPS:
                m = 2 * i + mm
                src, c0 = (br, 0) if what == 3 else (gate, what * D)
                blocks.append(_tiles(src, slice(c0 + m * P, c0 + (m + 1) * P), np))
        blocks += [_tiles(a["w_o"][l], slice(m * P, (m + 1) * P), np) for m in range(KC)]
        blocks += ffn("ffn2")
    blocks += [np.zeros((P, KC * P), np.float32)] * 2
    assert len(blocks) == 2 * (PAIR_MEM + L * PAIRS + 1)
    return np.stack(blocks)


def constants(np):
    f = np.float32
    c = np.zeros((P, NCST), f)
    pos = np.concatenate([np.arange(T_PROMPT), np.tile(1024 + np.arange(DEC_T), DEC_B)]).astype(f)
    inv = np.power(f(500000.0), -np.arange(8, dtype=f) * f(2.0 / 16)).astype(f)
    ang = (pos[None, :] * inv[:, None]).astype(f)
    p = np.arange(P)
    d = p % HD
    c[:, C_COS:C_COS + T] = 1.0
    for r in range(P):
        if d[r] < 16:
            c[r, C_COS:C_COS + T] = np.cos(ang[d[r] % 8])
            c[r, C_SIN:C_SIN + T] = np.sin(ang[d[r] % 8]) * (-1 if d[r] < 8 else 1)
            c[r + (8 if d[r] < 8 else -8), C_ROT + r] = 1.0
    c[:, C_ID:C_ID + P] = np.eye(P)
    c[:, C_ONES:C_ONES + P] = 1.0 / D
    j = np.arange(P)[None, :]
    i = p[:, None]
    c[:, C_MASK:C_MASK + P] = np.where(j > i, 0, NEG)
    c[:, C_MASK + P:C_MASK + 2 * P] = np.where(j <= i, 0, NEG)
    t = (p % 8)[:, None]
    b = (p // 64)[:, None]
    c[:, C_MSC:C_MSC + P] = np.where(j > t, 0, NEG)
    for tile in range(4):
        kb, kt = np.arange(64)[None, :] // 8, np.arange(64)[None, :] % 8
        c[:, C_MSN + tile * 64:C_MSN + (tile + 1) * 64] = np.where((kb == 2 * tile + b) & (kt <= t), 0, NEG)
    for ch in range(2):
        w = np.where(p < 64, 2, 4) * (4 if ch else 1)
        c[:, C_INVW + ch] = 1.0 / w
        c[:, C_TAB + 16 * ch:C_TAB + 16 * ch + 16] = 1.0 / np.minimum(w[:, None], np.arange(16)[None, :] + 1)
    return c


def kernel(**inputs):
    import numpy as np
    import concourse.bacc as bacc
    from concourse.bass_utils import run_bass_kernel_spmd as run

    a = {n: np.asarray(v) for n, v in inputs.items()}

    def fm(x):
        return x.reshape(x.shape[0], -1, P).transpose(2, 1, 0)

    xs = a["x_sample"].reshape(DEC_B * DEC_T, D)
    par = np.zeros((L, P, NPAR), np.float32)
    for l in range(L):
        for n in range(3):
            for j, w in enumerate("gb"):
                par[l, :, 16 * n + 8 * j:16 * n + 8 * j + 8] = a[f"ln{n + 1}_{w}"][l].reshape(KC, P).T
        for c in range(2):
            for h in range(2):
                par[l, h * 64:h * 64 + 64, P_MIX + c * P + h * 64:P_MIX + c * P + h * 64 + 64] = a["pool_mix"][l, 2 * c + h]
        par[l, :, P_SCALE:P_SCALE + 2] = a["pool_scale"][l].reshape(2, P).T
        par[l, :, P_SINK:P_SINK + 8] = a["attn_sink"][l][None, :]
        par[l, :, P_SROW] = a["attn_sink"][l][(np.arange(P) // 8) % 8]
    mk = a["cache_mem_k"].reshape(L, DEC_B, N_MEM, 2, P)
    mv = a["cache_mem_v"].reshape(L, DEC_B, 2, P, 256)
    kc = a["cache_swa_k"].reshape(L, DEC_B, WIN, P)
    vc = a["cache_swa_v"].reshape(L, DEC_B, WIN, P)
    sp = a["state_pool"].reshape(L, DEC_B, POOL_STATE, 2, P)
    arrays = {
        "wblk": pack_weights(a, np),
        "x0": np.concatenate([fm(a["x_prompt"][0]), fm(xs)], axis=2),
        "mem0": fm(a["mem_prompt"][0]),
        "cst": constants(np),
        "par": par,
        "mks": mk.transpose(0, 4, 3, 1, 2).reshape(L, P, -1),
        "mvs": mv.transpose(0, 3, 2, 1, 4).reshape(L, P, -1),
        "kcs": kc.transpose(0, 3, 1, 2).reshape(L, P, -1),
        "vcs": vc.transpose(0, 2, 1, 3).reshape(L, P, -1),
        "sps": sp.transpose(0, 4, 3, 1, 2),
    }
    arrays = {n: np.ascontiguousarray(v) for n, v in arrays.items()}
    outs = {
        "y": (P, KC, T), "kT": (L, P, P + 64), "v": (L, P + 64, P), "poolp": (L, P, 2, POOL_STATE),
        "pools": (L, P, 2, DEC_B, POOL_STATE), "mk_out": (L, P, 512), "mv_out": (L, P, 512),
        "kc_out": (L, P, DEC_B, WIN - DEC_T), "vc_out": (L, WIN - DEC_T, DEC_B * P),
    }
    nc = bacc.Bacc("TRN2", target_bir_lowering=False, num_devices=1)
    args = [nc.dram_tensor("in_" + n, v.shape, F32, kind="ExternalInput").ap() for n, v in arrays.items()]
    args += [nc.dram_tensor("out_" + n, s, F32, kind="ExternalOutput").ap() for n, s in outs.items()]
    build(nc, *args)
    r = run(nc, [{"in_" + n: v for n, v in arrays.items()}], core_ids=[0]).results[0]
    r = {n: r["out_" + n] for n in outs}

    y = r["y"].transpose(2, 1, 0).reshape(T, D)
    kT = r["kT"].transpose(0, 2, 1)
    v = r["v"]
    pools = r["pools"].transpose(0, 3, 4, 2, 1).reshape(L, DEC_B, POOL_STATE, 256)
    kco = r["kc_out"].transpose(0, 2, 3, 1)
    vco = r["vc_out"].reshape(L, WIN - DEC_T, DEC_B, P).transpose(0, 2, 1, 3)
    return (
        y[:T_PROMPT][None], y[T_PROMPT:].reshape(DEC_B, DEC_T, D),
        kT[:, :P].reshape(L, 1, WIN, 2, HD), v[:, :P].reshape(L, 1, WIN, 2, HD),
        r["poolp"].transpose(0, 3, 2, 1).reshape(L, 1, POOL_STATE, 256),
        r["mk_out"].reshape(L, P, 2, N_MEM).transpose(0, 3, 2, 1).reshape(L, 1, N_MEM, 4, HD),
        r["mv_out"].reshape(L, P, 2, 256).transpose(0, 2, 1, 3).reshape(L, 1, N_MEM, 4, HD),
        np.concatenate([kco, kT[:, P:].reshape(L, DEC_B, DEC_T, P)], axis=2).reshape(L, DEC_B, WIN, 2, HD),
        np.concatenate([vco, v[:, P:].reshape(L, DEC_B, DEC_T, P)], axis=2).reshape(L, DEC_B, WIN, 2, HD),
        pools,
    )
```
